# Optimizing a Trainium2 kernel written in Bass

```python
import math
import jax, jax.numpy as jnp
from jax import lax
import numpy as np
import jax
import jax.numpy as jnp

D_MODEL = 1024
BATCH = 1
SEQ = 256
DEPTH = 1

MIX_WIDTH = D_MODEL
CONV_WIDTH = MIX_WIDTH // 2
FFT_WIDTH = MIX_WIDTH - CONV_WIDTH
GROUP_DIM = 64
CONV_HEADS = CONV_WIDTH // GROUP_DIM
FFT_GROUPS = FFT_WIDTH // GROUP_DIM
IN_PROJ_WIDTH = 3 * CONV_WIDTH + FFT_WIDTH
CONV_K = 3
MEM_LEN = 256
XATTN_HEADS = 4
XATTN_HEAD_DIM = D_MODEL // XATTN_HEADS
N_EXPERTS = 32
TOP_K = 4
D_EXPERT = D_MODEL
SWIGLU_LIMIT = 7.0
SWIGLU_ALPHA = 1.702
ROW_BLOCK = 128
EPS = 1e-5


def rmsnorm(x, g):
    xf = x.astype(jnp.float32)
    y = xf * lax.rsqrt(jnp.mean(xf * xf, axis=-1, keepdims=True) + EPS)
    return (y * g.astype(jnp.float32)).astype(x.dtype)

def short_conv3(u, w):
    up = jnp.pad(u, ((0, 0), (1, 1), (0, 0)))
    return w[0] * up[:, :-2] + w[1] * up[:, 1:-1] + w[2] * up[:, 2:]

def hybrid_mixer(h, w_in, conv_w, g_conv_out, g_fft_out, w_out):
    bsz, s, _ = h.shape
    z = h @ w_in
    b_gate = z[..., :CONV_WIDTH]
    c_gate = z[..., CONV_WIDTH:2 * CONV_WIDTH]
    v = z[..., 2 * CONV_WIDTH:3 * CONV_WIDTH]
    u = z[..., 3 * CONV_WIDTH:]
    y_conv = b_gate * short_conv3(c_gate * v, conv_w)
    uf = u.astype(jnp.float32).reshape(bsz, s, FFT_GROUPS, GROUP_DIM)
    y_fft = jnp.fft.fftn(uf, axes=(1, 3), norm="ortho").real
    y_fft = y_fft.reshape(bsz, s, FFT_WIDTH).astype(h.dtype)
    y = jnp.concatenate([rmsnorm(y_conv, g_conv_out), rmsnorm(y_fft, g_fft_out)], axis=-1)
    return y @ w_out

def memory_cross_attention(h, mem_n, w_q, w_k, w_v, w_o):
    bsz, s, d = h.shape
    m = mem_n.shape[1]
    q = (h @ w_q).reshape(bsz, s, XATTN_HEADS, XATTN_HEAD_DIM)
    k = (mem_n @ w_k).reshape(bsz, m, XATTN_HEADS, XATTN_HEAD_DIM)
    v = (mem_n @ w_v).reshape(bsz, m, XATTN_HEADS, XATTN_HEAD_DIM)
    scores = jnp.einsum('bshd,bmhd->bhsm', q, k).astype(jnp.float32) * (XATTN_HEAD_DIM ** -0.5)
    p = jax.nn.softmax(scores, axis=-1).astype(v.dtype)
    o = jnp.einsum('bhsm,bmhd->bshd', p, v).reshape(bsz, s, d)
    return o @ w_o

def moe_ffn(h, w_router, b_router, w_gate_up, b_gate_up, w_down, b_down):
    bsz, s, d = h.shape
    t = bsz * s
    hf = h.reshape(t, d)
    logits = (hf @ w_router).astype(jnp.float32) + b_router.astype(jnp.float32)
    top_v, top_i = lax.top_k(logits, TOP_K)
    top_w = jax.nn.softmax(top_v, axis=-1)
    n_assign = t * TOP_K
    flat_e = top_i.reshape(n_assign)
    flat_tok = jnp.repeat(jnp.arange(t, dtype=jnp.int32), TOP_K)
    flat_w = top_w.reshape(n_assign)
    order = jnp.argsort(flat_e)
    sorted_e = flat_e[order]
    counts = jnp.bincount(flat_e, length=N_EXPERTS)
    padded = ((counts + ROW_BLOCK - 1) // ROW_BLOCK) * ROW_BLOCK
    start = jnp.cumsum(counts) - counts
    pad_end = jnp.cumsum(padded)
    pad_start = pad_end - padded
    dest = pad_start[sorted_e] + jnp.arange(n_assign) - start[sorted_e]
    n_blocks = -(-n_assign // ROW_BLOCK) + N_EXPERTS
    n_rows = n_blocks * ROW_BLOCK
    row_tok = jnp.full((n_rows,), t, dtype=jnp.int32).at[dest].set(flat_tok[order])
    row_w = jnp.zeros((n_rows,), jnp.float32).at[dest].set(flat_w[order])
    block_e = jnp.minimum(
        jnp.searchsorted(pad_end, jnp.arange(n_blocks) * ROW_BLOCK, side='right'), N_EXPERTS - 1)
    h_pad = jnp.concatenate([hf, jnp.zeros((1, d), hf.dtype)], axis=0)
    xs = h_pad[row_tok].reshape(n_blocks, ROW_BLOCK, d)

    def expert_block(args):
        xb, e = args
        gu = xb @ w_gate_up[e] + b_gate_up[e]
        gate = jnp.minimum(gu[:, :D_EXPERT], SWIGLU_LIMIT)
        up = jnp.clip(gu[:, D_EXPERT:], -SWIGLU_LIMIT, SWIGLU_LIMIT)
        glu = gate * jax.nn.sigmoid(SWIGLU_ALPHA * gate)
        return ((up + 1.0) * glu) @ w_down[e] + b_down[e]

    out = lax.map(expert_block, (xs, block_e)).reshape(n_rows, d)
    y = jnp.zeros((t + 1, d), out.dtype).at[row_tok].add(out * row_w[:, None].astype(out.dtype))
    return y[:t].reshape(bsz, s, d)

def first_inputs(seed: int = 0) -> dict:
    key = jax.random.key(seed)
    ks = jax.random.split(key, 24)
    f32 = jnp.float32

    def nrm(k, shape, scale):
        return jax.random.normal(k, shape, f32) * scale

    def gain(k, shape):
        return 1.0 + 0.02 * jax.random.normal(k, shape, f32)

    L = DEPTH
    return {
        "x": nrm(ks[0], (BATCH, SEQ, D_MODEL), 1.0),
        "mem": nrm(ks[1], (BATCH, MEM_LEN, D_MODEL), 1.0),
        "norm_mix": gain(ks[2], (L, D_MODEL)),
        "w_in": nrm(ks[3], (L, D_MODEL, IN_PROJ_WIDTH), D_MODEL ** -0.5),
        "conv_w": nrm(ks[4], (L, CONV_K, CONV_WIDTH), CONV_K ** -0.5),
        "g_conv_out": gain(ks[5], (L, CONV_WIDTH)),
        "g_fft_out": gain(ks[6], (L, FFT_WIDTH)),
        "w_out": nrm(ks[7], (L, MIX_WIDTH, D_MODEL), MIX_WIDTH ** -0.5),
        "norm_xattn": gain(ks[8], (L, D_MODEL)),
        "norm_mem": gain(ks[9], (L, D_MODEL)),
        "w_q": nrm(ks[10], (L, D_MODEL, D_MODEL), D_MODEL ** -0.5),
        "w_k": nrm(ks[11], (L, D_MODEL, D_MODEL), D_MODEL ** -0.5),
        "w_v": nrm(ks[12], (L, D_MODEL, D_MODEL), D_MODEL ** -0.5),
        "w_o": nrm(ks[13], (L, D_MODEL, D_MODEL), D_MODEL ** -0.5),
        "norm_ffn": gain(ks[14], (L, D_MODEL)),
        "w_router": nrm(ks[15], (L, D_MODEL, N_EXPERTS), D_MODEL ** -0.5),
        "b_router": nrm(ks[16], (L, N_EXPERTS), 0.01),
        "w_gate_up": nrm(ks[17], (L, N_EXPERTS, D_MODEL, 2 * D_EXPERT), D_MODEL ** -0.5),
        "b_gate_up": nrm(ks[18], (L, N_EXPERTS, 2 * D_EXPERT), 0.02),
        "w_down": nrm(ks[19], (L, N_EXPERTS, D_EXPERT, D_MODEL), D_EXPERT ** -0.5),
        "b_down": nrm(ks[20], (L, N_EXPERTS, D_MODEL), 0.02),
        "norm_final": gain(ks[21], (D_MODEL,)),
    }

def first_block(x, mem, norm_mix, w_in, conv_w, g_conv_out, g_fft_out, w_out,
              norm_xattn, norm_mem, w_q, w_k, w_v, w_o, norm_ffn, w_router, b_router,
              w_gate_up, b_gate_up, w_down, b_down, norm_final):
    for l in range(DEPTH):
        h = rmsnorm(x, norm_mix[l])
        x = x + hybrid_mixer(h, w_in[l], conv_w[l], g_conv_out[l], g_fft_out[l], w_out[l])
        h = rmsnorm(x, norm_xattn[l])
        mem_n = rmsnorm(mem, norm_mem[l])
        x = x + memory_cross_attention(h, mem_n, w_q[l], w_k[l], w_v[l], w_o[l])
        h = rmsnorm(x, norm_ffn[l])
        x = x + moe_ffn(h, w_router[l], b_router[l], w_gate_up[l], b_gate_up[l], w_down[l], b_down[l])
    return rmsnorm(x, norm_final)


DEPTH_2 = 4

N_MIXERS = 3
ROPE_THETA = 500000.0
EPS_2 = 1e-6
Q_BLOCK = 128
MASK_VALUE = -1e30

A_HEADS = 8
A_HEAD_DIM = D_MODEL // A_HEADS // 2
A_V_DIM = 2 * A_HEAD_DIM
A_ROT = A_HEAD_DIM // 4

B_HEADS = 16
B_Q_RANK = 384
B_KV_RANK = 256
B_NOPE = 64
B_ROPE = 32
B_V = 64

C_GROUPS = ((128, 1), (512, 4), (2048, 16))
C_HEADS = 16
C_HEAD_DIM = 64
C_ROT = C_HEAD_DIM // 4
C_BLOCK = 64

FFN_DIM = -(-8 * D_MODEL // (3 * 256)) * 256

N_A = (DEPTH_2 + 2) // 3
N_B = (DEPTH_2 + 1) // 3
N_C = DEPTH_2 // 3


def rms_norm(x, g):
    xf = x.astype(jnp.float32)
    y = xf * lax.rsqrt(jnp.mean(xf * xf, axis=-1, keepdims=True) + EPS_2) * g.astype(jnp.float32)
    return y.astype(x.dtype)

def rope_tables(seq_len, rot_dim):
    pos = jnp.arange(seq_len, dtype=jnp.float32)
    inv = ROPE_THETA ** (-jnp.arange(0, rot_dim, 2, dtype=jnp.float32) / rot_dim)
    ang = pos[:, None] * inv[None, :]
    return jnp.cos(ang), jnp.sin(ang)

def apply_rope(x, cos, sin):
    r = cos.shape[-1]
    shape = (x.shape[1],) + (1,) * (x.ndim - 3) + (r,)
    c = cos.reshape(shape)
    s = sin.reshape(shape)
    xf = x[..., :2 * r].astype(jnp.float32)
    x1, x2 = xf[..., :r], xf[..., r:]
    rot = jnp.concatenate([x1 * c - x2 * s, x2 * c + x1 * s], axis=-1).astype(x.dtype)
    return jnp.concatenate([rot, x[..., 2 * r:]], axis=-1)

def _to_blocks(t):
    b, h, s, d = t.shape
    return t.reshape(b, h, s // Q_BLOCK, Q_BLOCK, d).transpose(2, 0, 1, 3, 4)

def _from_blocks(t):
    nb, b, h, q, d = t.shape
    return t.transpose(1, 2, 0, 3, 4).reshape(b, h, nb * q, d)

def diff_attention(h, w_qkv, lam_q1, lam_k1, lam_q2, lam_k2, subln, w_o, lambda_init, cos, sin):
    B, S, _ = h.shape
    qk_w = 2 * A_HEADS * A_HEAD_DIM
    qkv = h @ w_qkv
    q = qkv[..., :qk_w].reshape(B, S, 2 * A_HEADS, A_HEAD_DIM)
    k = qkv[..., qk_w:2 * qk_w].reshape(B, S, 2 * A_HEADS, A_HEAD_DIM)
    v = qkv[..., 2 * qk_w:].reshape(B, S, A_HEADS, A_V_DIM)
    q = (apply_rope(q, cos, sin) * (A_HEAD_DIM ** -0.5)).transpose(0, 2, 1, 3)
    k = apply_rope(k, cos, sin).transpose(0, 2, 1, 3)
    v = v.transpose(0, 2, 1, 3)
    lam = (jnp.exp(jnp.sum(lam_q1.astype(jnp.float32) * lam_k1.astype(jnp.float32)))
           - jnp.exp(jnp.sum(lam_q2.astype(jnp.float32) * lam_k2.astype(jnp.float32)))
           + lambda_init)

    def block(qb):
        s = jnp.einsum('bhqd,bhkd->bhqk', qb, k).astype(jnp.float32)
        p = jax.nn.softmax(s, axis=-1).reshape(B, A_HEADS, 2, qb.shape[2], S)
        a = p[:, :, 0] - lam * p[:, :, 1]
        return jnp.einsum('bhqk,bhkd->bhqd', a.astype(v.dtype), v)

    o = _from_blocks(lax.map(block, _to_blocks(q)))
    o = rms_norm(o, subln) * (1.0 - lambda_init)
    o = o.transpose(0, 2, 1, 3).reshape(B, S, A_HEADS * A_V_DIM)
    return o @ w_o

def latent_attention(h, w_a, q_norm, kv_norm, w_qb, w_kvb, w_o, cos, sin):
    B, S, _ = h.shape
    a = h @ w_a
    q_lat = rms_norm(a[..., :B_Q_RANK], q_norm)
    kv_lat = rms_norm(a[..., B_Q_RANK:B_Q_RANK + B_KV_RANK], kv_norm)
    k_rope = apply_rope(a[..., B_Q_RANK + B_KV_RANK:], cos, sin)
    scale = (B_NOPE + B_ROPE) ** -0.5
    q = (q_lat @ w_qb).reshape(B, S, B_HEADS, B_NOPE + B_ROPE)
    q_nope = (q[..., :B_NOPE] * scale).transpose(0, 2, 1, 3)
    q_rope = (apply_rope(q[..., B_NOPE:], cos, sin) * scale).transpose(0, 2, 1, 3)
    kv = (kv_lat @ w_kvb).reshape(B, S, B_HEADS, B_NOPE + B_V)
    k_nope = kv[..., :B_NOPE].transpose(0, 2, 1, 3)
    v = kv[..., B_NOPE:].transpose(0, 2, 1, 3)

    def block(qs):
        qn, qr = qs
        s = (jnp.einsum('bhqd,bhkd->bhqk', qn, k_nope)
             + jnp.einsum('bhqr,bkr->bhqk', qr, k_rope)).astype(jnp.float32)
        p = jax.nn.softmax(s, axis=-1)
        return jnp.einsum('bhqk,bhkd->bhqd', p.astype(v.dtype), v)

    o = _from_blocks(lax.map(block, (_to_blocks(q_nope), _to_blocks(q_rope))))
    o = o.transpose(0, 2, 1, 3).reshape(B, S, B_HEADS * B_V)
    return o @ w_o

def _dilated_group(q, k, v, window, dilation):
    B, S, H, hd = q.shape
    radius = (window // 2) // dilation
    L = S // dilation
    nb = -(-L // C_BLOCK)
    Lp = nb * C_BLOCK

    def phase(t):
        t = t.reshape(B, L, dilation, H, hd).transpose(0, 2, 3, 1, 4)
        return jnp.pad(t, ((0, 0), (0, 0), (0, 0), (0, Lp - L), (0, 0)))

    def band(t):
        t = jnp.pad(phase(t), ((0, 0), (0, 0), (0, 0), (C_BLOCK, C_BLOCK), (0, 0)))
        t = t.reshape(B, dilation, H, nb + 2, C_BLOCK, hd)
        return jnp.concatenate([t[:, :, :, :-2], t[:, :, :, 1:-1], t[:, :, :, 2:]], axis=-2)

    qb = phase(q).reshape(B, dilation, H, nb, C_BLOCK, hd)
    kb, vb = band(k), band(v)
    blk = jnp.arange(nb)[:, None]
    qpos = blk * C_BLOCK + jnp.arange(C_BLOCK)[None, :]
    kpos = (blk - 1) * C_BLOCK + jnp.arange(3 * C_BLOCK)[None, :]
    mask = ((jnp.abs(qpos[:, :, None] - kpos[:, None, :]) <= radius)
            & (kpos[:, None, :] >= 0) & (kpos[:, None, :] < L))
    s = jnp.einsum('bphnqd,bphnkd->bphnqk', qb, kb).astype(jnp.float32)
    s = jnp.where(mask, s, MASK_VALUE)
    lse = jax.nn.logsumexp(s, axis=-1, keepdims=True)
    p = jnp.exp(s - lse)
    o = jnp.einsum('bphnqk,bphnkd->bphnqd', p.astype(v.dtype), vb)
    o = o.reshape(B, dilation, H, Lp, hd)[:, :, :, :L].transpose(0, 3, 1, 2, 4).reshape(B, S, H, hd)
    lse = lse[..., 0].reshape(B, dilation, H, Lp)[..., :L].transpose(0, 3, 1, 2).reshape(B, S, H)
    return o, lse

def dilated_attention(h, w_qkv, w_o, cos, sin):
    B, S, _ = h.shape
    G = len(C_GROUPS)
    qkv = (h @ w_qkv).reshape(B, S, G, 3, C_HEADS, C_HEAD_DIM)
    q = apply_rope(qkv[:, :, :, 0], cos, sin) * (C_HEAD_DIM ** -0.5)
    k = apply_rope(qkv[:, :, :, 1], cos, sin)
    v = qkv[:, :, :, 2]
    outs, lses = [], []
    for g, (window, dilation) in enumerate(C_GROUPS):
        o_g, l_g = _dilated_group(q[:, :, g], k[:, :, g], v[:, :, g], window, dilation)
        outs.append(o_g)
        lses.append(l_g)
    wts = jax.nn.softmax(jnp.stack(lses, axis=0), axis=0)
    o = jnp.sum(wts[..., None].astype(v.dtype) * jnp.stack(outs, axis=0), axis=0)
    return o.reshape(B, S, C_HEADS * C_HEAD_DIM) @ w_o

def swiglu(h, w_gu, w_out):
    gu = h @ w_gu
    return (jax.nn.silu(gu[..., :FFN_DIM]) * gu[..., FFN_DIM:]) @ w_out

def _w(k, shape, fan_in):
    return jax.random.normal(k, shape, jnp.float32) * (fan_in ** -0.5)

def _gain(k, shape):
    return 1.0 + 0.02 * jax.random.normal(k, shape, jnp.float32)

def second_inputs(seed: int = 0) -> dict:
    key = jax.random.key(seed)
    ks = jax.random.split(key, 21)
    D = D_MODEL
    a_qkv = 2 * 2 * A_HEADS * A_HEAD_DIM + A_HEADS * A_V_DIM
    c_qkv = len(C_GROUPS) * 3 * C_HEADS * C_HEAD_DIM
    return {
        'x': jax.random.normal(ks[0], (BATCH, SEQ, D), jnp.float32),
        'attn_norm': _gain(ks[1], (DEPTH_2, D)),
        'ffn_norm': _gain(ks[2], (DEPTH_2, D)),
        'final_norm': _gain(ks[3], (D,)),
        'a_w_qkv': _w(ks[4], (N_A, D, a_qkv), D),
        'a_lambda_q1': 0.1 * jax.random.normal(ks[5], (N_A, A_HEAD_DIM), jnp.float32),
        'a_lambda_k1': 0.1 * jax.random.normal(ks[6], (N_A, A_HEAD_DIM), jnp.float32),
        'a_lambda_q2': 0.1 * jax.random.normal(ks[7], (N_A, A_HEAD_DIM), jnp.float32),
        'a_lambda_k2': 0.1 * jax.random.normal(ks[8], (N_A, A_HEAD_DIM), jnp.float32),
        'a_subln': _gain(ks[9], (N_A, A_V_DIM)),
        'a_w_o': _w(ks[10], (N_A, A_HEADS * A_V_DIM, D), A_HEADS * A_V_DIM),
        'b_w_a': _w(ks[11], (N_B, D, B_Q_RANK + B_KV_RANK + B_ROPE), D),
        'b_q_norm': _gain(ks[12], (N_B, B_Q_RANK)),
        'b_kv_norm': _gain(ks[13], (N_B, B_KV_RANK)),
        'b_w_qb': _w(ks[14], (N_B, B_Q_RANK, B_HEADS * (B_NOPE + B_ROPE)), B_Q_RANK),
        'b_w_kvb': _w(ks[15], (N_B, B_KV_RANK, B_HEADS * (B_NOPE + B_V)), B_KV_RANK),
        'b_w_o': _w(ks[16], (N_B, B_HEADS * B_V, D), B_HEADS * B_V),
        'c_w_qkv': _w(ks[17], (N_C, D, c_qkv), D),
        'c_w_o': _w(ks[18], (N_C, C_HEADS * C_HEAD_DIM, D), C_HEADS * C_HEAD_DIM),
        'f_w_gu': _w(ks[19], (DEPTH_2, D, 2 * FFN_DIM), D),
        'f_w_out': _w(ks[20], (DEPTH_2, FFN_DIM, D), FFN_DIM),
    }

def second_block(x, attn_norm, ffn_norm, final_norm, a_w_qkv, a_lambda_q1, a_lambda_k1, a_lambda_q2,
              a_lambda_k2, a_subln, a_w_o, b_w_a, b_q_norm, b_kv_norm, b_w_qb, b_w_kvb, b_w_o,
              c_w_qkv, c_w_o, f_w_gu, f_w_out):
    S = x.shape[1]
    cos_p, sin_p = rope_tables(S, A_ROT)
    cos_b, sin_b = rope_tables(S, B_ROPE)
    for i in range(DEPTH_2):
        m, j = i % N_MIXERS, i // N_MIXERS
        h = rms_norm(x, attn_norm[i])
        if m == 0:
            lambda_init = 0.8 - 0.6 * math.exp(-0.3 * i)
            mix = diff_attention(h, a_w_qkv[j], a_lambda_q1[j], a_lambda_k1[j], a_lambda_q2[j],
                                 a_lambda_k2[j], a_subln[j], a_w_o[j], lambda_init, cos_p, sin_p)
        elif m == 1:
            mix = latent_attention(h, b_w_a[j], b_q_norm[j], b_kv_norm[j], b_w_qb[j], b_w_kvb[j],
                                   b_w_o[j], cos_b, sin_b)
        else:
            mix = dilated_attention(h, c_w_qkv[j], c_w_o[j], cos_p, sin_p)
        x = x + mix
        x = x + swiglu(rms_norm(x, ffn_norm[i]), f_w_gu[i], f_w_out[i])
    return rms_norm(x, final_norm)


def setup_inputs(seed=0):
    out = dict(first_inputs(seed))
    for name, value in second_inputs(seed + 1).items():
        if name != "x":
            out[name + "_2"] = value
    return out


def reference(
    x, mem, norm_mix, w_in, conv_w, g_conv_out, g_fft_out, w_out, norm_xattn, norm_mem, w_q,
    w_k, w_v, w_o, norm_ffn, w_router, b_router, w_gate_up, b_gate_up, w_down, b_down,
    norm_final, attn_norm_2, ffn_norm_2, final_norm_2, a_w_qkv_2, a_lambda_q1_2, a_lambda_k1_2,
    a_lambda_q2_2, a_lambda_k2_2, a_subln_2, a_w_o_2, b_w_a_2, b_q_norm_2, b_kv_norm_2,
    b_w_qb_2, b_w_kvb_2, b_w_o_2, c_w_qkv_2, c_w_o_2, f_w_gu_2, f_w_out_2,
):
    x = first_block(
        x, mem, norm_mix, w_in, conv_w, g_conv_out, g_fft_out, w_out, norm_xattn, norm_mem, w_q,
        w_k, w_v, w_o, norm_ffn, w_router, b_router, w_gate_up, b_gate_up, w_down, b_down,
        norm_final,
    )
    return second_block(
        x, attn_norm_2, ffn_norm_2, final_norm_2, a_w_qkv_2, a_lambda_q1_2, a_lambda_k1_2,
        a_lambda_q2_2, a_lambda_k2_2, a_subln_2, a_w_o_2, b_w_a_2, b_q_norm_2, b_kv_norm_2,
        b_w_qb_2, b_w_kvb_2, b_w_o_2, c_w_qkv_2, c_w_o_2, f_w_gu_2, f_w_out_2,
    )


_drawn_inputs = setup_inputs


def setup_inputs(seed=0):
    import zlib

    import numpy as np

    out = dict(_drawn_inputs(seed))
    spreads = {}
    factors = {'norm_xattn': 8.0,
     'b_gate_up': 3.304,
     'b_down': 2.682,
     'final_norm_2': 2.829,
     'a_lambda_q2_2': 3.265,
     'a_subln_2': 3.262,
     'b_q_norm_2': 8.0,
     'b_kv_norm_2': 8.0}
    for name, (base, spread) in spreads.items():
        noise = np.random.default_rng([zlib.crc32(name.encode()), seed]).standard_normal(out[name].shape)
        drawn = base * np.exp(spread * noise) if base else spread * noise
        out[name] = jnp.asarray(drawn.astype(out[name].dtype))
    for name, factor in factors.items():
        out[name] = (out[name] * factor).astype(out[name].dtype)
    return out
```

```python
import math
import numpy as np
import concourse.bass as bass
from concourse import mybir
from contextlib import ExitStack

F32 = mybir.dt.float32
I32 = mybir.dt.int32
ALU = mybir.AluOpType
ACT = mybir.ActivationFunctionType
AX = mybir.AxisListType

D = 1024
S = 256
P = 128
KB = D // P
NT = S // P
HALF = D // 2
CB = HALF // P
GROUP = 64
E = 32
TOP = 4
CAP = P
ITEMS = E + 8
FB = 22
EPS1, EPS2 = 1e-5, 1e-6
LIMIT, ALPHA = 7.0, 1.702
R = 6
UW = 2048
MASKED = -1e30

CONST = {}


def const_table():
    cols = []

    def put(name, a):
        a = np.asarray(a, np.float64).reshape(P, -1)
        CONST[name] = (sum(c.shape[1] for c in cols), a.shape[1])
        cols.append(a)

    put("ones", np.ones((P, P)))
    put("ident", np.eye(P))
    put("before", np.triu(np.ones((P, P)), 1))
    put("slot", np.tile(np.arange(2 * P), (P, 1)))
    put("expert", np.arange(P)[:, None])
    put("rot_ac", rotation(64, 0, 8))
    put("cs_ac", rope_table(64, 0, 8))
    put("rot_b", rotation(32, 0, 16))
    put("cs_b", rope_table(32, 0, 16))
    t = np.arange(S)
    ang = 2 * np.pi * ((t[:, None] * t[None, :]) % S) / S
    cs = np.concatenate([np.cos(ang), np.sin(ang)], 1) / math.sqrt(S)
    put("dft_seq", cs.reshape(NT, P, 2 * S).transpose(1, 0, 2))
    c = np.arange(GROUP)
    ang = 2 * np.pi * ((c[:, None] * c[None, :]) % GROUP) / GROUP
    two = np.eye(P // GROUP)
    put("dft_cos", np.kron(two, np.cos(ang)) / math.sqrt(GROUP))
    put("dft_nsin", np.kron(two, -np.sin(ang)) / math.sqrt(GROUP))
    q, k = np.arange(S)[:, None], np.arange(S)[None, :]
    near = np.abs(q - k) <= 64
    for name, ok in (("mask0", near), ("mask1", (q - k) % 4 == 0), ("mask2", (q - k) % 16 == 0)):
        m = np.where(ok, 0.0, MASKED * 8.0)
        put(name, m.reshape(NT, P, S).transpose(1, 0, 2))
    return np.concatenate(cols, 1).astype(np.float32)


def rotation(head, at, r):
    m = np.zeros((head, head))
    for i in range(r):
        m[at + r + i, at + i] = -1.0
        m[at + i, at + r + i] = 1.0
    return np.kron(np.eye(P // head), m)


def rope_table(head, at, r):
    pos = np.arange(S, dtype=np.float32)
    inv = (np.float32(500000.0) ** (-np.arange(0, 2 * r, 2, dtype=np.float32) / np.float32(2 * r))).astype(np.float32)
    ang = (pos[:, None] * inv[None, :]).astype(np.float32).astype(np.float64)
    c, s = np.ones((head, S)), np.zeros((head, S))
    c[at:at + r], c[at + r:at + 2 * r] = np.cos(ang).T, np.cos(ang).T
    s[at:at + r], s[at + r:at + 2 * r] = np.sin(ang).T, np.sin(ang).T
    c, s = np.tile(c, (P // head, 1)), np.tile(s, (P // head, 1))
    return np.concatenate([c, c, s, s], 1)


CONSTS = const_table()

PARAM_SIZES = [
    ("norm_mix", 8), ("norm_mem", 8), ("norm_xattn", 8), ("norm_ffn", 8), ("norm_final", 8),
    ("g_conv", 4), ("g_fft", 4), ("conv_w", 12), ("attn", 32), ("ffn", 32), ("final2", 8),
    ("q_norm", 3), ("kv_norm", 2), ("subln", 2), ("b_router", 64), ("lam", 8 * 64),
]
PARAM = {}
_at = 0
for _n, _w in PARAM_SIZES:
    PARAM[_n] = _at
    _at += _w
NPARAM = _at

PRE = {"w_in": 0, "w_k": 8, "w_v": 12, "w_out": 16, "w_q": 20, "w_o": 24}
N_PRE = 28
POST = {}
_at = 0
LAYER_UNITS = {"a_qkv": 12, "a_o": 4, "b_a": 3, "b_q": 6, "b_k": 4, "b_v": 4, "b_o": 4, "c_qkv": 36, "c_o": 4}
LAYERS = [["a_qkv", "a_o"], ["b_a", "b_q", "b_k", "b_v", "b_o"], ["c_qkv", "c_o"], ["a_qkv", "a_o"]]
FFN_UNITS = FB + FB // 2
for _l, _names in enumerate(LAYERS):
    for _n in _names:
        POST[_n, _l] = _at
        _at += LAYER_UNITS[_n]
    POST["ffn", _l] = _at
    _at += FFN_UNITS
N_POST = _at


def program(nc, x, mem, consts, params, pre, post, router, bgu, bdown, wgu, wdn, out):
    ctx = ExitStack()
    with ctx:
        def sb(name, shape, dt=F32):
            return ctx.enter_context(nc.sbuf_tensor(name, shape, dt))

        def sem(name):
            return ctx.enter_context(nc.semaphore(name))

        xt = sb("xt", [P, KB, S])
        ht = sb("ht", [P, KB, S])
        sq = sb("sq", [P, KB, S])
        ring = sb("ring", [P, R, UW])
        con = sb("con", [P, CONSTS.shape[1]])
        par = sb("par", [P, NPARAM])
        big = sb("big", [P, 9 * 2048])
        prob = sb("prob", [P, 2, 1536])
        probt = sb("probt", [P, 1536])
        root = sb("root", [P, S])
        rstd = sb("rstd", [P, S])
        eps1 = sb("eps1", [P, 1])
        eps2 = sb("eps2", [P, 1])
        small = sb("small", [P, 64])
        items = sb("items", [1, 1 + 2 * ITEMS], I32)
        bank = [ctx.enter_context(nc.psum_tensor(f"bank{b}", [P, 512], F32)) for b in range(8)]

        def c(name):
            a, n = CONST[name]
            return con[:, a:a + n]

        def g(name, k=0):
            return par[:, PARAM[name] + k:PARAM[name] + k + 1]

        def blocks(a, w=S):
            return a.rearrange("p (b n) -> p b n", n=w)

        def area(at, n):
            return big[:, at * 256:(at + n) * 256]

        ones, ident = c("ones"), c("ident")

        s_x, s_mem, s_const = sem("x_loaded"), sem("mem_loaded"), sem("const_loaded")
        s_eps = sem("eps_set")
        pre_in = [sem(f"pre_in{i}") for i in range(R)]
        pre_done = sem("pre_unit_done")
        moe_in = [sem(f"moe_in{i}") for i in range(R)]
        moe_done = sem("moe_unit_done")
        moe_over = sem("moe_over")
        post_in = [sem(f"post_in{i}") for i in range(R)]
        post_done = sem("post_unit_done")
        s_evac = sem("tile_evacuated")
        s_xadd = sem("residual_added")
        s_sq, s_sum, s_root, s_rstd, s_norm = (sem(n) for n in ("norm_squared", "norm_summed", "norm_root", "norm_rstd", "norm_ready"))
        s_link = sem("dve_step")
        s_raw, s_rot = sem("rope_raw"), sem("rope_rotated")
        s_fpq, s_fpe, s_fy = sem("fft_seq_done"), sem("fft_seq_copied"), sem("fft_group_done")
        s_sc, s_max, s_exp, s_prob, s_tr, s_pt, s_pv, s_o = (sem("att_" + n) for n in ("scores", "max", "exp", "prob", "turned", "probt", "pv", "out"))
        s_sig = sem("ffn_sigmoid")
        s_out = sem("out_written")

        block = ctx.enter_context(nc.Block())

        class Phase:
            def __init__(self, arrived, done, first_wait=None):
                self.arrived, self.done = arrived, done

        PRE_PH, POST_PH = Phase(pre_in, pre_done), Phase(post_in, post_done)

        def wait_unit(eng, ph, u, i=0, per=0):
            eng.wait_ge(ph.arrived[u % R], 16 * (u // R + 1) + i * (16 * per // R))

        def slot(u, k):
            return ring[:, u % R, :].rearrange("p (k n) -> p k n", k=k)

        NORMS, norm_base = [], []

        def add_norm(name, src, dst, gain, n, eps, src_wait, dst_wait):
            norm_base.append(sum(len(j["src"]) for j in NORMS))
            NORMS.append(dict(name=name, src=src, dst=dst, gain=gain, n=n, eps=eps, src_wait=src_wait, dst_wait=dst_wait))
            return len(NORMS) - 1

        def norm_ready(eng, j, k=None):
            n = len(NORMS[j]["src"]) if k is None else k + 1
            eng.wait_ge(s_norm, norm_base[j] + n)

        def norm_act(act, j):
            m = NORMS[j]
            if j >= 1:
                act.wait_ge(s_sum, j)
            for k, a in enumerate(m["src"]):
                m["src_wait"](act, k)
                act.activation(sq[:, k, :], a, ACT.Square).then_inc(s_sq, 1)
            act.wait_ge(s_sum, j + 1)
            if j >= 1:
                act.wait_ge(s_rstd, j)
            act.activation(root[:, :], bank[0][:, 0:S], ACT.Sqrt, bias=m["eps"][:, 0:1], scale=1.0 / m["n"]).then_inc(s_root, 1)

        def norm_pe(pe, j):
            m = NORMS[j]
            if j >= 1:
                pe.wait_ge(s_root, j)
            for k in range(len(m["src"])):
                pe.wait_ge(s_sq, norm_base[j] + k + 1)
                mm = pe.matmul(bank[0][:, 0:S], ones, sq[:, k, :], start=(k == 0), stop=(k == len(m["src"]) - 1))
            mm.then_inc(s_sum, 1)

        def norm_dve(dve, j):
            m = NORMS[j]
            if j >= 1:
                dve.wait_ge(s_norm, norm_base[j])
            dve.wait_ge(s_root, j + 1)
            dve.reciprocal(rstd[:, :], root[:, :]).then_inc(s_rstd, 1)
            dve.wait_ge(s_rstd, j + 1)
            m["dst_wait"](dve)
            for k, a in enumerate(m["src"]):
                m["src_wait"](dve, k)
                dve.scalar_tensor_tensor(m["dst"][k], a, g(m["gain"][0], m["gain"][1] + k), rstd[:, :], ALU.mult, ALU.mult).then_inc(s_norm, 1)

        class Link:
            n = 0

            def __call__(self, ins, dve):
                ins.then_inc(s_link, 1)
                self.n += 1
                dve.wait_ge(s_link, self.n)

        link = Link()

        JOBS = {}
        tiles_so_far = [0]

        def add_tiles(name, n):
            JOBS[name] = tiles_so_far[0]
            tiles_so_far[0] += n
            return JOBS[name]

        def tile_bank(t):
            return bank[4 + t % 4]

        def tile_free(pe, t, i=0, per=0):
            if t >= 4:
                pe.wait_ge(s_evac, t - 3 + i * per)

        def project(pe, ph, u, t, kind, src, kc=KB, i=0, per=0):
            wait_unit(pe, ph, u, i, per)
            tile_free(pe, t, i, per)
            w = ring[:, u % R, 0:kc * 256].rearrange("p (k n) -> p k n", k=kc)
            o = tile_bank(t)
            for h in range(2):
                for k in range(kc):
                    if kind == "T":
                        mm = pe.matmul(o[:, h * S:(h + 1) * S], w[:, k, h * P:(h + 1) * P], src[k], start=(k == 0), stop=(k == kc - 1))
                    else:
                        mm = pe.matmul(o[:, h * S:(h + 1) * S], src[k][:, h * P:(h + 1) * P], w[:, k, :], start=(k == 0), stop=(k == kc - 1))
            mm.then_inc(ph.done, 1)

        def tile_done(eng, ph, u, i=0, per=0):
            eng.wait_ge(ph.done, u + 1 + i * per)

        hts = [ht[:, k, :] for k in range(KB)]
        xts = [xt[:, k, :] for k in range(KB)]

        z = [area(k, 1) for k in range(12)]
        u_tok = area(12, 4).rearrange("p (t n) -> p t n", t=NT)
        pq = area(16, 8).rearrange("p (b n) -> p b n", n=2 * S)
        yf = [area(24 + k, 1) for k in range(CB)]
        yc = [area(28 + k, 1) for k in range(CB)]
        cv = big[:, 32 * 256:32 * 256 + CB * (S + 2)].rearrange("p (b n) -> p b n", n=S + 2)
        mt = [area(40 + k, 1) for k in range(KB)]
        kx = [area(48 + k, 1) for k in range(KB)]
        vx = area(56, 8).rearrange("p (t n) -> p t n", t=NT)
        qx = [area(64 + k, 1) for k in range(KB)]
        memt = blocks(area(40, 8))
        raw = probt[:, 0:1024].rearrange("p (a n) -> p a n", a=2)
        m1 = prob[:, 0, 0:512]
        m2 = prob[:, 0, 512:1024]

        xadds = [0]
        STAGES = []

        def stage(pe=None, act=None, dve=None, sp=None):
            STAGES.append(dict(pe=pe, act=act, dve=dve, sp=sp))

        def loads(ph, dram, u0, n, width=UW):
            def run(sp):
                for u in range(u0, u0 + n):
                    if u >= R:
                        sp.wait_ge(ph.done, u - R + 1)
                    elif ph is POST_PH and u == 0:
                        sp.wait_ge(moe_over, 1)
                    sp.dma_start(ring[:, u % R, 0:width], dram[u, :, 0:width]).then_inc(ph.arrived[u % R], 16)
            return run

        def copy_stage(name, ph, dram, u0, kinds, src, src_ready, dests, kc=KB):
            n = len(kinds)
            t0 = add_tiles(name, n)

            def pe_(pe):
                src_ready(pe)
                for i in range(n):
                    project(pe, ph, u0 + i, t0 + i, kinds[i], src, kc)

            def dve_(dve):
                for i in range(n):
                    tile_done(dve, ph, u0 + i)
                    dve.tensor_copy(dests[i], tile_bank(t0 + i)[:, :].rearrange("p (a n) -> p a n", a=2)).then_inc(s_evac, 1)
            stage(pe=pe_, dve=dve_, sp=loads(ph, dram, u0, n, kc * 256))
            return t0 + n

        def resid_stage(name, ph, dram, u0, src, src_ready):
            t0 = add_tiles(name, 4)
            x0 = xadds[0]
            xadds[0] += 4

            def pe_(pe):
                src_ready(pe)
                for i in range(4):
                    project(pe, ph, u0 + i, t0 + i, "T", src)

            def dve_(dve):
                for i in range(4):
                    tile_done(dve, ph, u0 + i)
                    if x0 == 0:
                        dve.wait_ge(s_x, 16)
                    o = xt[:, 2 * i:2 * i + 2, :]
                    dve.tensor_tensor(o, o, tile_bank(t0 + i)[:, :].rearrange("p (a n) -> p a n", a=2), ALU.add).then_inc(s_evac, 1)
            stage(pe=pe_, dve=dve_, sp=loads(ph, dram, u0, 4))
            return t0

        def norm_stage(*a, **k):
            j = add_norm(*a, **k)
            stage(pe=lambda pe: norm_pe(pe, j), act=lambda act: norm_act(act, j), dve=lambda dve: norm_dve(dve, j))
            return j

        def after_tiles(t0):
            return lambda eng, k: eng.wait_ge(s_evac, t0 + k // 2 + 1)

        def none(*a):
            pass

        att_count = dict(sc=0, mx=0, exp=0, prob=0, tr=0, pt=0, pv=0, o=0)

        def attention(name, heads, groups, twins, q, k, v, pv_parts, o_dst, scale, ready, masks=None, coef=None, o_free=None):
            base = dict(att_count)
            att_count["sc"] += heads
            att_count["mx"] += heads
            att_count["exp"] += heads
            att_count["prob"] += heads
            att_count["tr"] += heads
            att_count["pt"] += heads
            pairs = pv_parts == "half"
            att_count["pv"] += heads
            att_count["o"] += heads // 2 if pairs else heads
            nb = groups * twins
            W = groups * S

            def sbank(h, j):
                return bank[j] if nb > 1 else bank[h % 2]

            def tbank(h, j):
                return bank[3 + j] if groups > 1 else bank[3 + h % 2]

            def obank(h):
                n = h // 2 if pairs else h
                return bank[6 + n % 2]

            def scores(pe, h):
                if nb > 1 and h >= 1:
                    if masks:
                        pe.wait_ge(s_max, base["mx"] + h)
                    else:
                        pe.wait_ge(s_exp, base["exp"] + h)
                if nb == 1 and h >= 2:
                    pe.wait_ge(s_exp, base["exp"] + h - 1)
                for j in range(nb):
                    for t in range(NT):
                        parts = q(h, j, t)
                        rhs = k(h, j)
                        for a in range(len(parts)):
                            mm = pe.matmul(sbank(h, j)[:, t * S:(t + 1) * S], parts[a], rhs[a], start=(a == 0), stop=(a == len(parts) - 1))
                mm.then_inc(s_sc, 1)

            def pr(h, w=0):
                return prob[:, h % 2, w * 512:w * 512 + NT * W].rearrange("p (t n) -> p t n", t=NT)

            def turn(pe, h):
                pe.wait_ge(s_prob, base["prob"] + h + 1)
                if groups > 1 and h >= 1:
                    pe.wait_ge(s_pt, base["pt"] + h)
                if groups == 1 and h >= 2:
                    pe.wait_ge(s_pt, base["pt"] + h - 1)
                for ch in range(W // P):
                    for t in range(NT):
                        mm = pe.transpose(tbank(h, ch // 2)[:, (ch % 2) * S + t * P:(ch % 2) * S + (t + 1) * P],
                                          pr(h)[:, t, ch * P:(ch + 1) * P], ident)
                mm.then_inc(s_tr, 1)

            def times_v(pe, h):
                pe.wait_ge(s_pt, base["pt"] + h + 1)
                n = h // 2 if pairs else h
                if n >= 2 and not (pairs and h % 2):
                    pe.wait_ge(s_o, base["o"] + n - 1)
                pt = probt[:, 0:NT * W].rearrange("p (c n) -> p c n", n=S)
                for part in range(2 if pv_parts == "two" else 1):
                    for ch in range(W // P):
                        if pairs:
                            o = obank(h)[64 * (h % 2):64 * (h % 2) + 64, 0:S]
                        else:
                            o = obank(h)[:, part * S:(part + 1) * S]
                        mm = pe.matmul(o, v(h, ch, part), pt[:, ch, :], start=(ch == 0), stop=(ch == W // P - 1))
                mm.then_inc(s_pv, 1)

            def pe_(pe):
                ready(pe)
                scores(pe, 0)
                if heads > 1:
                    scores(pe, 1)
                for h in range(heads):
                    turn(pe, h)
                    if h + 2 < heads:
                        scores(pe, h + 2)
                    times_v(pe, h)

            sm = small

            def col(h, what, w=0):
                a = (h % 2) * 24 + {"max": 0, "sum": 8, "r": 16}[what] + 2 * w
                return a

            def maxes(dve, h):
                dve.wait_ge(s_sc, base["sc"] + h + 1)
                if h >= 2:
                    dve.wait_ge(s_tr, base["tr"] + h - 1)
                if masks:
                    for j in range(groups):
                        mins = dve.tensor_tensor(pr(h)[:, :, j * S:(j + 1) * S], bank[j][:, :].rearrange("p (t n) -> p t n", t=NT), masks[j], ALU.add)
                    link(mins, dve)
                    src = [pr(h)]
                else:
                    src = [sbank(h, w)[:, :].rearrange("p (t n) -> p t n", t=NT) for w in range(twins)]
                for w, a in enumerate(src):
                    m = col(h, "max", w)
                    mins = dve.tensor_reduce(sm[:, m:m + 2], a, AX.X, ALU.max)
                link(mins, dve)
                m = col(h, "max")
                dve.tensor_scalar(sm[:, m:m + 2 * twins], sm[:, m:m + 2 * twins], -scale, None, ALU.mult).then_inc(s_max, 1)

            def exps(act, h):
                act.wait_ge(s_max, base["mx"] + h + 1)
                if h >= 2:
                    act.wait_ge(s_prob, base["prob"] + h - 1)
                    act.wait_ge(s_tr, base["tr"] + h - 1)
                for w in range(twins):
                    for t in range(NT):
                        src = pr(h)[:, t, :] if masks else sbank(h, w)[:, t * S:(t + 1) * S]
                        m, s_ = col(h, "max", w) + t, col(h, "sum", w) + t
                        ins = act.activation(pr(h, w)[:, t, :], src, ACT.Exp, bias=sm[:, m:m + 1], scale=scale, accum_out=sm[:, s_:s_ + 1])
                ins.then_inc(s_exp, 1)

            def norms(dve, h):
                dve.wait_ge(s_exp, base["exp"] + h + 1)
                s_, r = col(h, "sum"), col(h, "r")
                link(dve.reciprocal(sm[:, r:r + 2 * twins], sm[:, s_:s_ + 2 * twins]), dve)
                if twins == 2:
                    link(dve.tensor_scalar(sm[:, r + 2:r + 4], sm[:, r + 2:r + 4], coef, None, ALU.mult), dve)
                    for t in range(NT):
                        ins = dve.tensor_scalar(pr(h, 1)[:, t, :], pr(h, 1)[:, t, :], sm[:, r + 2 + t:r + 3 + t], None, ALU.mult)
                    link(ins, dve)
                    for t in range(NT):
                        ins = dve.scalar_tensor_tensor(pr(h)[:, t, :], pr(h)[:, t, :], sm[:, r + t:r + t + 1], pr(h, 1)[:, t, :], ALU.mult, ALU.add)
                else:
                    for t in range(NT):
                        ins = dve.tensor_scalar(pr(h)[:, t, :], pr(h)[:, t, :], sm[:, r + t:r + t + 1], None, ALU.mult)
                ins.then_inc(s_prob, 1)

            def turned(act, h):
                act.wait_ge(s_tr, base["tr"] + h + 1)
                if h >= 1:
                    act.wait_ge(s_pv, base["pv"] + h)
                for j in range(groups):
                    ins = act.activation(probt[:, j * 512:(j + 1) * 512], tbank(h, j)[:, :], ACT.Copy)
                ins.then_inc(s_pt, 1)

            def outs(dve, n):
                if o_free is not None and n == 0:
                    o_free(dve)
                dve.wait_ge(s_pv, base["pv"] + (2 * n + 2 if pairs else n + 1))
                b = bank[6 + n % 2]
                if pv_parts == "two":
                    src = b[:, :].rearrange("p (a n) -> p a n", a=2)
                else:
                    src = b[:, 0:S]
                dve.tensor_copy(o_dst(n), src).then_inc(s_o, 1)

            def dve_(dve):
                maxes(dve, 0)
                for h in range(heads):
                    if h + 1 < heads:
                        maxes(dve, h + 1)
                    norms(dve, h)
                    if h >= 1:
                        if not pairs:
                            outs(dve, h - 1)
                        elif h % 2 == 0:
                            outs(dve, h // 2 - 1)
                outs(dve, heads // 2 - 1 if pairs else heads - 1)

            def act_(act):
                exps(act, 0)
                for h in range(heads):
                    if h + 1 < heads:
                        exps(act, h + 1)
                    turned(act, h)
            stage(pe=pe_, act=act_, dve=dve_)
            return base["o"] + (heads // 2 if pairs else heads)


        rope_count = [0]

        def rope_stage(name, ph, dram, u0, spec, src, src_ready, rot, tabs, kc=KB, times=1, step=0):
            n = len(spec)
            t0 = add_tiles(name, n * times)
            r0 = rope_count[0]
            per_r = sum(1 for x_ in spec if x_[1])
            rope_count[0] += per_r * times
            R_ = rot
            cos2, sin2 = tabs[:, 0:512], tabs[:, 512:1024]

            def index(l):
                return sum(1 for x_ in spec[:l] if x_[1])

            turned_at = [l for l in range(n) if spec[l][1]]

            def wait_two_before(eng, l, i):
                a = index(l)
                if a >= 2:
                    eng.wait_ge(s_evac, t0 + turned_at[a - 2] + 1 + i * n)
                elif r0 or times > 1 or t0:
                    eng.wait_ge(s_evac, t0 + i * n)

            def place(l, i):
                kind, turned_, at, _ = spec[l]
                if kind == "T":
                    a = big[:, bass.ds(i * (step * 256) + at * 256, 512)] if times > 1 else big[:, at * 256:at * 256 + 512]
                    return a.rearrange("p (a n) -> p a n", a=2)
                m, o = at
                if times > 1:
                    a = big[:, bass.ds(i * (step * 256) + m * 256, 2048)]
                else:
                    a = big[:, m * 256:m * 256 + 2048]
                return a.rearrange("p (t n) -> p t n", t=NT)[:, :, o * 256:(o + 1) * 256]

            def rot_one(pe, l, i):
                r = r0 + index(l)
                pe.wait_ge(s_raw, r + 1 + i * per_r)
                wait_two_before(pe, l, i)
                pe.matmul(bank[1 + r % 2][:, :], R_, raw[:, r % 2, :], start=True, stop=True).then_inc(s_rot, 1)

            def body_pe(pe, i):
                for l in range(n):
                    project(pe, ph, u0 + l, t0 + l, spec[l][0], src, kc, i, n)
                    if l >= 1 and spec[l - 1][1]:
                        rot_one(pe, l - 1, i)
                if spec[n - 1][1]:
                    rot_one(pe, n - 1, i)

            def body_act(act, i):
                for l in turned_at:
                    r = r0 + index(l)
                    tile_done(act, ph, u0 + l, i, n)
                    wait_two_before(act, l, i)
                    act.activation(raw[:, r % 2, :], tile_bank(t0 + l)[:, :], ACT.Copy).then_inc(s_raw, 1)

            def body_dve(dve, i, base, dyn):
                k = 0
                for l in range(n):
                    b2 = tile_bank(t0 + l)[:, :].rearrange("p (a n) -> p a n", a=2)
                    if not spec[l][1]:
                        tile_done(dve, ph, u0 + l, i, n)
                        dve.tensor_copy(place(l, i), b2).then_inc(s_evac, 1)
                        continue
                    r = r0 + index(l)
                    dve.wait_ge(s_raw, r + 1 + i * per_r)
                    dve.wait_ge(s_evac, t0 + l + i * n)
                    dve.tensor_tensor(m1, raw[:, r % 2, :], cos2, ALU.mult)
                    dve.wait_ge(s_rot, r + 1 + i * per_r)
                    dve.tensor_tensor(m2, bank[1 + r % 2][:, :], sin2, ALU.mult).then_inc(s_link, 1)
                    k += 1
                    dve.wait_ge(s_link, base + k + dyn)
                    m1b, m2b = (m_.rearrange("p (a n) -> p a n", a=2) for m_ in (m1, m2))
                    dve.tensor_tensor(place(l, i), m1b, m2b, ALU.add).then_inc(s_evac, 1)

            def pe_(pe):
                src_ready(pe)
                if times == 1:
                    body_pe(pe, 0)
                else:
                    with pe.Fori(0, times) as i:
                        body_pe(pe, i)

            def act_(act):
                if times == 1:
                    body_act(act, 0)
                else:
                    with act.Fori(0, times) as i:
                        body_act(act, i)

            def dve_(dve):
                base = link.n
                if times == 1:
                    body_dve(dve, 0, base, 0)
                else:
                    with dve.Fori(0, times) as i:
                        body_dve(dve, i, base, i * per_r)
                link.n = base + per_r * times

            def sp_(sp):
                if times == 1:
                    return loads(ph, dram, u0, n, kc * 256)(sp)
                with sp.Fori(0, times) as i:
                    for l in range(n):
                        u = u0 + l
                        sp.wait_ge(ph.done, u - R + 1 + i * n)
                        sp.dma_start(ring[:, u % R, :], dram[bass.ds(i * n + u, 1), :, :].rearrange("a p n -> (a p) n")).then_inc(ph.arrived[u % R], 16)
            stage(pe=pe_, act=act_, dve=dve_, sp=sp_)
            return t0 + n * times

        hid = area(0, 4).rearrange("p (b n) -> p b n", n=S)
        sgm = area(4, 2).rearrange("p (b n) -> p b n", n=S)
        gsg = area(6, 2).rearrange("p (b n) -> p b n", n=S)
        sig_count = [0]

        def ffn_stage(l, src_ready):
            u0 = POST["ffn", l]
            t0 = add_tiles(("ffn", l), FB)
            g0 = sig_count[0]
            sig_count[0] += FB
            x0 = add_tiles(("ffn_x", l), 4)

            def gu(q):
                return u0 + (q if q < 2 else 2 + 3 * (q // 2 - 1) + q % 2)

            def ou(j):
                return u0 + 4 + 3 * j if j < FB // 2 - 1 else u0 + FFN_UNITS - 1

            def out_unit(pe, j, i=0, per=0, tper=0):
                u = ou(j)
                wait_unit(pe, POST_PH, u, i, per)
                pe.wait_ge(s_evac, t0 + 2 * j + 2 + i * tper)
                w = ring[:, u % R, :].rearrange("p (k n) -> p k n", k=2)
                for k in range(2):
                    for d in range(KB):
                        mm = pe.matmul(bank[d // 2][:, (d % 2) * S:(d % 2 + 1) * S], w[:, k, d * P:(d + 1) * P], hid[:, (2 * j + k) % 4, :],
                                       start=(j == 0 and k == 0 and d % 2 == 0), stop=(j == FB // 2 - 1 and k == 1), skip_group_check=True)
                mm.then_inc(post_done, 1)

            def step_pe(pe, j, i=0, per=0, tper=0):
                for q in (2 * j, 2 * j + 1):
                    project(pe, POST_PH, gu(q), t0 + q, "T", hts, KB, i, per) if tper == 0 else project2(pe, gu(q), t0 + q, i)
                if j >= 1:
                    out_unit(pe, j - 1, i, per, tper)

            def project2(pe, u, t, i):
                wait_unit(pe, POST_PH, u, i, 6)
                pe.wait_ge(s_evac, t - 3 + i * 4)
                w = ring[:, u % R, :].rearrange("p (k n) -> p k n", k=KB)
                for h in range(2):
                    for k in range(KB):
                        mm = pe.matmul(tile_bank(t)[:, h * S:(h + 1) * S], w[:, k, h * P:(h + 1) * P], hts[k], start=(k == 0), stop=(k == KB - 1))
                mm.then_inc(post_done, 1)

            def pe_(pe):
                src_ready(pe)
                step_pe(pe, 0)
                step_pe(pe, 1)
                with pe.Fori(0, 4) as i:
                    step_pe(pe, 2, i, 6, 4)
                    step_pe(pe, 3, i, 6, 4)
                step_pe(pe, FB // 2 - 1)
                out_unit(pe, FB // 2 - 1)

            def piece_act(act, q, i=0):
                act.wait_ge(post_done, gu(q) + 1 + i * 6)
                if g0 + q >= 2:
                    act.wait_ge(s_evac, t0 + q - 1 + i * 4)
                act.activation(sgm[:, q % 2, :], tile_bank(t0 + q)[:, 0:S], ACT.Sigmoid).then_inc(s_sig, 1)

            def piece_dve(dve, q, i=0, k=0, base=0, dyn=0):
                dve.wait_ge(s_sig, g0 + q + 1 + i * 4)
                dve.tensor_tensor(gsg[:, q % 2, :], tile_bank(t0 + q)[:, 0:S], sgm[:, q % 2, :], ALU.mult).then_inc(s_link, 1)
                dve.wait_ge(s_link, base + k + 1 + dyn)
                if q >= 4:
                    dve.wait_ge(post_done, ou(q // 2 - 2) + 1 + i * 6)
                dve.tensor_tensor(hid[:, q % 4, :], gsg[:, q % 2, :], tile_bank(t0 + q)[:, S:2 * S], ALU.mult).then_inc(s_evac, 1)

            def act_(act):
                for q in range(4):
                    piece_act(act, q)
                with act.Fori(0, 4) as i:
                    for q in range(4, 8):
                        piece_act(act, q, i)
                for q in range(FB - 2, FB):
                    piece_act(act, q)

            def dve_(dve):
                base = link.n
                for q in range(4):
                    piece_dve(dve, q, 0, q, base)
                with dve.Fori(0, 4) as i:
                    for q in range(4, 8):
                        piece_dve(dve, q, i, q, base, i * 4)
                for q in range(FB - 2, FB):
                    piece_dve(dve, q, 0, q, base)
                link.n = base + FB
                dve.wait_ge(post_done, u0 + FFN_UNITS)
                for b in range(4):
                    o = xt[:, 2 * b:2 * b + 2, :]
                    dve.tensor_tensor(o, o, bank[b][:, :].rearrange("p (a n) -> p a n", a=2), ALU.add).then_inc(s_evac, 1)

            def sp_(sp):
                loads(POST_PH, post, u0, 5)(sp)
                with sp.Fori(0, 4) as i:
                    for n_ in range(6):
                        u = u0 + 5 + n_
                        sp.wait_ge(post_done, u - R + 1 + i * 6)
                        sp.dma_start(ring[:, u % R, :], post[bass.ds(i * 6 + u, 1), :, :].rearrange("a p n -> (a p) n")).then_inc(post_in[u % R], 16)
                loads(POST_PH, post, u0 + 29, 4)(sp)
            stage(pe=pe_, act=act_, dve=dve_, sp=sp_)
            return x0

        def first_sp(sp):
            sp.dma_start(xt[:, :, :], x).then_inc(s_x, 16)
            sp.dma_start(con[:, :], consts).then_inc(s_const, 16)
            sp.dma_start(par[:, :], params).then_inc(s_const, 16)
            sp.dma_start(memt, mem).then_inc(s_mem, 16)

        def first_dve(dve):
            dve.memset(eps1[:, :], EPS1).then_inc(s_eps, 1)
            dve.memset(eps2[:, :], EPS2).then_inc(s_eps, 1)
            dve.wait_ge(s_const, 32)

        def first_act(act):
            act.wait_ge(s_const, 32)
            act.wait_ge(s_eps, 2)
        stage(pe=lambda pe: pe.wait_ge(s_const, 32), act=first_act, dve=first_dve, sp=first_sp)

        lamw = sb("lamw", [P, 64])
        lam_e = sb("lam_e", [P, 8])
        lam_neg = sb("lam_neg", [P, 2])
        sub_g = sb("sub_g", [P, 2])
        s_lam, s_lame, s_lamn = sem("lambda_sums"), sem("lambda_exps"), sem("lambda_ready")
        INIT = [0.8 - 0.6 * math.exp(-0.3 * i) for i in (0, 3)]

        def lam_dve(dve):
            a = PARAM["lam"]
            for n in range(4):
                lo = a + n * 128
                link(dve.tensor_tensor(lamw[:, :], par[:, lo:lo + 64], par[:, lo + 64:lo + 128], ALU.mult), dve)
                ins = dve.tensor_reduce(lam_e[:, n:n + 1], lamw[:, :], AX.X, ALU.add)
                link(ins, dve)
            dve.memset(small[:, 60:61], 0.0).then_inc(s_lam, 1)
            dve.wait_ge(s_lame, 1)
            for l in range(2):
                link(dve.tensor_tensor(lam_neg[:, l:l + 1], lam_e[:, 5 + 2 * l:6 + 2 * l], lam_e[:, 4 + 2 * l:5 + 2 * l], ALU.subtract), dve)
                dve.tensor_scalar(lam_neg[:, l:l + 1], lam_neg[:, l:l + 1], -INIT[l], None, ALU.add).then_inc(s_lamn, 1)
                dve.tensor_scalar(sub_g[:, l:l + 1], g("subln", l), 1.0 - INIT[l], None, ALU.mult).then_inc(s_lamn, 1)
            dve.wait_ge(s_lamn, 4)

        def lam_act(act):
            act.wait_ge(s_lam, 1)
            act.activation(lam_e[:, 4:8], lam_e[:, 0:4], ACT.Exp).then_inc(s_lame, 1)
        stage(dve=lam_dve, act=lam_act)

        wait_x = lambda eng, k: eng.wait_ge(s_x, 16)

        n_mix = norm_stage("mix", xts, hts, ("norm_mix", 0), D, eps1, wait_x, none)
        dests = [blocks(area(2 * i, 2)) for i in range(6)] + [u_tok[:, :, 0:256], u_tok[:, :, 256:512]]
        t_in = copy_stage("w_in", PRE_PH, pre, PRE["w_in"], "TTTTTTNN", hts, lambda pe: norm_ready(pe, n_mix), dests)

        s_conv = sem("conv_ready")

        def fft_pe(pe):
            pe.wait_ge(s_evac, t_in)
            for b in range(CB):
                for t in range(NT):
                    mm = pe.matmul(bank[b][:, :], u_tok[:, t, b * P:(b + 1) * P], c("dft_seq").rearrange("p (t n) -> p t n", t=NT)[:, t, :], start=(t == 0), stop=(t == 1))
                mm.then_inc(s_fpq, 1)
            for b in range(CB):
                pe.wait_ge(s_fpe, b + 1)
                pe.matmul(bank[4 + b][:, 0:S], c("dft_cos"), pq[:, b, 0:S], start=True, stop=False)
                pe.matmul(bank[4 + b][:, 0:S], c("dft_nsin"), pq[:, b, S:2 * S], start=False, stop=True).then_inc(s_fy, 1)

        def fft_act(act):
            act.wait_ge(s_sum, 1)
            for b in range(CB):
                act.wait_ge(s_fpq, b + 1)
                act.activation(pq[:, b, :], bank[b][:, :], ACT.Copy).then_inc(s_fpe, 1)
            for b in range(CB):
                act.wait_ge(s_fy, b + 1)
                act.activation(yf[b], bank[4 + b][:, 0:S], ACT.Copy).then_inc(s_fpe, 1)

        def conv_dve(dve):
            dve.memset(cv[:, :, 0:1], 0.0)
            dve.memset(cv[:, :, S + 1:S + 2], 0.0)
            dve.wait_ge(s_evac, t_in)
            link(dve.tensor_tensor(cv[:, :, 1:S + 1], blocks(area(4, 4)), blocks(area(8, 4)), ALU.mult), dve)
            for b in range(CB):
                dve.tensor_scalar(yc[b], cv[:, b, 0:S], g("conv_w", b), None, ALU.mult)
            for w in (1, 2):
                link(dve.memset(small[:, 60:61], 0.0), dve)
                for b in range(CB):
                    dve.scalar_tensor_tensor(yc[b], cv[:, b, w:w + S], g("conv_w", 4 * w + b), yc[b], ALU.mult, ALU.add)
            link(dve.memset(small[:, 60:61], 0.0), dve)
            dve.tensor_tensor(blocks(area(28, 4)), blocks(area(28, 4)), blocks(area(0, 4)), ALU.mult).then_inc(s_conv, 1)
        stage(pe=fft_pe, act=fft_act, dve=conv_dve)

        n_mem = norm_stage("mem", mt, mt, ("norm_mem", 0), D, eps1, lambda eng, k: eng.wait_ge(s_mem, 16), none)
        copy_stage("w_k", PRE_PH, pre, PRE["w_k"], "TTTT", mt, lambda pe: norm_ready(pe, n_mem), [blocks(area(48 + 2 * i, 2)) for i in range(4)])
        copy_stage("w_v", PRE_PH, pre, PRE["w_v"], "NNNN", mt, none, [vx[:, :, i * 256:(i + 1) * 256] for i in range(4)])
        n_conv = norm_stage("conv", yc, hts[0:4], ("g_conv", 0), HALF, eps1, lambda eng, k: eng.wait_ge(s_conv, 1), none)
        n_fft = norm_stage("fft", yf, hts[4:8], ("g_fft", 0), HALF, eps1, lambda eng, k: eng.wait_ge(s_fpe, CB + k + 1), none)
        t = resid_stage("w_out", PRE_PH, pre, PRE["w_out"], hts, lambda pe: norm_ready(pe, n_fft))

        n_xa = norm_stage("xattn", xts, hts, ("norm_xattn", 0), D, eps1, after_tiles(t), none)
        t_q = copy_stage("w_q", PRE_PH, pre, PRE["w_q"], "TTTT", hts, lambda pe: norm_ready(pe, n_xa), [blocks(area(64 + 2 * i, 2)) for i in range(4)])
        o_n = attention("xattn", 4, 1, 1,
                        lambda h, j, t_: [qx[2 * h + a][:, t_ * P:(t_ + 1) * P] for a in range(2)],
                        lambda h, j: [kx[2 * h + a] for a in range(2)],
                        lambda h, ch, part: vx[:, ch, h * 256 + part * P:h * 256 + (part + 1) * P], "two",
                        lambda n: ht[:, 2 * n:2 * n + 2, :], 256 ** -0.5, lambda pe: pe.wait_ge(s_evac, t_q))
        t = resid_stage("w_o", PRE_PH, pre, PRE["w_o"], hts, lambda pe, o_n=o_n: pe.wait_ge(s_o, o_n))

        n_ffn = norm_stage("moe", xts, hts, ("norm_ffn", 0), D, eps1, after_tiles(t), none)
        h2 = area(0, 8).rearrange("p (t n) -> p t n", t=NT)
        xg = area(8, 4).rearrange("p (d n) -> p d n", n=CAP)
        sel = area(12, 1).rearrange("p (t n) -> p t n", t=NT)
        selw = area(13, 1).rearrange("p (t n) -> p t n", t=NT)
        selt = area(14, 1)
        mh = area(16, 4).rearrange("p (k n) -> p k n", n=CAP)
        yd = area(20, 4).rearrange("p (d n) -> p d n", n=CAP)
        ys = area(24, 4)
        g1 = area(28, 1).rearrange("p (a n) -> p a n", a=2)
        u1 = area(29, 1).rearrange("p (a n) -> p a n", a=2)
        sg = area(30, 1).rearrange("p (a n) -> p a n", a=2)
        gs = area(31, 1).rearrange("p (a n) -> p a n", a=2)
        gt = area(32, 1)

        def rt(k, w=64):
            return big[:, 40 * 256 + k * 64:40 * 256 + k * 64 + w].rearrange("p (t n) -> p t n", t=NT)

        logit, gates, more, equal, chosen, posm, tmp = (rt(k) for k in range(7))
        top8 = big[:, 47 * 256:47 * 256 + 16].rearrange("p (t n) -> p t n", t=NT)
        st_ = big[:, 47 * 256 + 16:47 * 256 + 32]
        eqs = [big[:, 48 * 256 + k * 96:48 * 256 + k * 96 + 96].rearrange("p (t n) -> p t n", t=NT) for k in range(2)]
        over = big[:, 50 * 256:50 * 256 + 64]

        bgu_s = sb("bgu_s", [P, 2 * KB * E])
        bdn_s = sb("bdn_s", [E, D])
        rtr_s = sb("rtr_s", [P, KB * E])
        fours = [sem(n) for n in ("moe_const", "turned_tokens", "tokens_copied", "logits", "logit_max", "logit_exp", "gate_step", "positions", "item_list", "items_ready")]
        s_mc, s_ht, s_h2, s_lg, s_lm, s_le, s_gt, s_ps, s_il, s_items = fours
        m_sel, m_gath, m_xg, m_g1, m_sig, m_hid, m_ycp, m_turn, m_ys, m_scat, m_add, m_link = (
            sem("moe_" + n) for n in ("selected", "gathered", "rows_copied", "gate_ready", "sigmoid", "hidden", "down_copied",
                                      "turned", "turned_copied", "scattered", "added", "dve_step"))
        s_gtp, s_gtc, s_bd = sem("gates_turned"), sem("gates_copied"), sem("down_bias_done")
        s_big = sem("residual_after_moe")
        PER = 12

        def moe_sp(sp):
            sp.dma_start(bgu_s[:, :], bgu).then_inc(s_mc, 16)
            sp.dma_start(bdn_s[:, :], bdown).then_inc(s_mc, 16)
            sp.dma_start(rtr_s[:, :], router).then_inc(s_mc, 16)
            sp.sem_inc(moe_done, R)

            def load(l, i, e):
                src = wgu[e, l] if l < KB else wdn[e, l - KB]
                sp.dma_start(ring[:, l % R, :], src).then_inc(moe_in[l % R], 16)
            for l in range(PER):
                if l < R:
                    sp.wait_ge(pre_done, N_PRE - R + 1 + (l - N_PRE % R) % R)
                else:
                    sp.wait_ge(moe_done, l + 1)
                load(l, 0, 0)
            sp.wait_ge(s_items, 1)
            n = sp.value_load(items[0:1, 0:1], min_val=E, max_val=ITEMS - 1)
            with sp.Fori(1, n) as i:
                e = sp.value_load(items[0:1, bass.ds(i + 1, 1)], min_val=0, max_val=E - 1)
                for l in range(PER):
                    sp.wait_ge(moe_done, l + 1 + i * PER)
                    src = wgu[bass.ds(e, 1), l] if l < KB else wdn[bass.ds(e, 1), l - KB]
                    sp.dma_start(ring[:, l % R, :], src.rearrange("a p n -> (a p) n")).then_inc(moe_in[l % R], 16)

        def moe_pe(pe):
            norm_ready(pe, n_ffn)
            for t_ in range(NT):
                for q_ in range(2):
                    for k in range(4):
                        mm = pe.transpose(bank[4 + 2 * t_ + q_][:, k * P:(k + 1) * P], ht[:, 4 * q_ + k, t_ * P:(t_ + 1) * P], ident)
                    mm.then_inc(s_ht, 1)
            pe.wait_ge(s_mc, 48)
            rw = rtr_s[:, :].rearrange("p (k n) -> p k n", n=E)
            for t_ in range(NT):
                for k in range(KB):
                    mm = pe.matmul(bank[1][:, t_ * E:(t_ + 1) * E], ht[:, k, t_ * P:(t_ + 1) * P], rw[:, k, :], start=(k == 0), stop=(k == KB - 1))
            mm.then_inc(s_lg, 1)
            pe.wait_ge(s_gt, 1)
            pe.matmul(bank[2][:, 0:E], c("before"), chosen[:, 0, :], start=True, stop=True)
            pe.matmul(bank[2][:, E:2 * E], ones, chosen[:, 0, :], start=True, stop=False)
            pe.matmul(bank[2][:, E:2 * E], c("before"), chosen[:, 1, :], start=False, stop=True)
            pe.matmul(bank[3][0:E, 0:2], chosen[:, 0, :], ones[:, 0:2], start=True, stop=False)
            pe.matmul(bank[3][0:E, 0:2], chosen[:, 1, :], ones[:, 0:2], start=False, stop=True).then_inc(s_ps, 1)
            pe.wait_ge(s_il, 1)
            pe.matmul(bank[1][0:E, 0:2], c("before")[0:E, 0:E], over[0:E, 0:2], start=True, stop=True).then_inc(s_ps, 1)
            pe.wait_ge(s_il, 2)
            pe.matmul(bank[3][0:1, 0:8], c("expert")[0:E, 0:1], over[0:E, 8:16], start=True, stop=True)
            pe.matmul(bank[1][0:1, 0:2], over[0:E, 0:1], ones[0:E, 0:2], start=True, stop=True).then_inc(s_ps, 1)
            pe.wait_ge(s_gt, 2)
            for t_ in range(NT):
                mm = pe.transpose(bank[2][0:E, t_ * P:(t_ + 1) * P], gates[:, t_, :], ident)
            mm.then_inc(s_gtp, 1)
            pe.wait_ge(s_gtc, 1)
            pe.wait_ge(s_items, 1)
            pe.wait_ge(s_h2, 4)
            n = pe.value_load(items[0:1, 0:1], min_val=E, max_val=ITEMS - 1)
            with pe.Fori(0, n) as i:
                pe.wait_ge(m_sel, i + 1)
                pe.wait_ge(m_ys, i + 1)
                pe.wait_ge(m_add, i + 1)
                for d in range(KB):
                    for t_ in range(NT):
                        pe.matmul(bank[d // 4][:, (d % 4) * CAP:(d % 4 + 1) * CAP], h2[:, t_, d * P:(d + 1) * P], sel[:, t_, :], start=(t_ == 0), stop=(t_ == 1))
                for t_ in range(NT):
                    mm = pe.transpose(bank[2][:, t_ * P:(t_ + 1) * P], selw[:, t_, :], ident)
                mm.then_inc(m_gath, 1)
                pe.wait_ge(m_xg, i + 1)
                for j in range(KB):
                    pe.wait_ge(moe_in[j % R], 16 * (j // R + 1) + i * 32)
                    pe.wait_ge(m_hid, j + 1 + i * KB)
                    w = slot(j, KB)
                    for h in range(2):
                        for k in range(KB):
                            mm = pe.matmul(bank[4 + j % 2][:, h * CAP:(h + 1) * CAP], w[:, k, h * P:(h + 1) * P], xg[:, k, :], start=(k == 0), stop=(k == KB - 1))
                    mm.then_inc(moe_done, 1)
                for m in range(4):
                    l = KB + m
                    pe.wait_ge(moe_in[l % R], 16 * (l // R + 1) + i * 32)
                    w = slot(l, 2)
                    for k2 in range(2):
                        k = 2 * m + k2
                        pe.wait_ge(m_hid, k + 3 + i * KB)
                        for d in range(KB):
                            mm = pe.matmul(bank[6 + d // 4][:, (d % 4) * CAP:(d % 4 + 1) * CAP], w[:, k2, d * P:(d + 1) * P], mh[:, k, :],
                                           start=(k == 0 and d % 4 == 0), stop=(k == KB - 1), skip_group_check=True)
                    mm.then_inc(moe_done, 1)
                pe.wait_ge(m_ycp, i + 1)
                for d in range(KB):
                    mm = pe.transpose(bank[d // 4][:, (d % 4) * P:(d % 4 + 1) * P], yd[:, d, :], ident)
                mm.then_inc(m_turn, 1)
                pe.wait_ge(m_ys, i + 2)
                for d in range(KB):
                    mm = pe.matmul(bank[(2, 3, 6, 7)[d // 2]][:, (d % 2) * S:(d % 2 + 1) * S], ys[:, d * P:(d + 1) * P], selt, start=True, stop=True)
                mm.then_inc(m_scat, 1)
            pe.wait_ge(s_bd, 1)
            for d in range(KB):
                mm = pe.matmul(bank[(2, 3, 6, 7)[d // 2]][:, (d % 2) * S:(d % 2 + 1) * S], bdn_s[:, d * P:(d + 1) * P], gt[0:E, :], start=True, stop=True)
            mm.then_inc(moe_over, 1)

        def moe_act(act):
            for q_ in range(4):
                act.wait_ge(s_ht, q_ + 1)
                act.activation(h2[:, q_ // 2, (q_ % 2) * 512:(q_ % 2 + 1) * 512], bank[4 + q_][:, :], ACT.Copy).then_inc(s_h2, 1)
            act.wait_ge(s_lm, 1)
            for t_ in range(NT):
                act.activation(gates[:, t_, :], logit[:, t_, :], ACT.Exp, bias=st_[:, 4 + t_:5 + t_]).then_inc(s_le, 1)
            act.wait_ge(s_gtp, 1)
            act.activation(gt[0:E, :], bank[2][0:E, 0:S], ACT.Copy).then_inc(s_gtc, 1)
            act.sem_inc(m_ys, 1)
            act.wait_ge(s_items, 1)
            n = act.value_load(items[0:1, 0:1], min_val=E, max_val=ITEMS - 1)
            with act.Fori(0, n) as i:
                act.wait_ge(m_gath, i + 1)
                act.activation(xg[:, 0:4, :], bank[0][:, :].rearrange("p (a n) -> p a n", n=CAP), ACT.Copy)
                act.activation(xg[:, 4:8, :], bank[1][:, :].rearrange("p (a n) -> p a n", n=CAP), ACT.Copy)
                act.activation(selt, bank[2][:, 0:S], ACT.Copy).then_inc(m_xg, 1)
                for j in range(KB):
                    act.wait_ge(m_g1, j + 1 + i * KB)
                    act.activation(sg[:, j % 2, :], g1[:, j % 2, :], ACT.Sigmoid, scale=ALPHA).then_inc(m_sig, 1)
                act.wait_ge(moe_done, R + PER + i * PER)
                act.activation(yd[:, 0:4, :], bank[6][:, :].rearrange("p (a n) -> p a n", n=CAP), ACT.Copy)
                act.activation(yd[:, 4:8, :], bank[7][:, :].rearrange("p (a n) -> p a n", n=CAP), ACT.Copy).then_inc(m_ycp, 1)
                act.wait_ge(m_turn, i + 1)
                act.activation(ys[:, 0:512], bank[0][:, :], ACT.Copy)
                act.activation(ys[:, 512:1024], bank[1][:, :], ACT.Copy).then_inc(m_ys, 1)

        def moe_dve(dve):
            dve.wait_ge(s_mc, 48)
            dve.wait_ge(s_lg, 1)
            br = par[:, PARAM["b_router"]:PARAM["b_router"] + 64].rearrange("p (t n) -> p t n", t=NT)
            link(dve.tensor_tensor(logit, bank[1][:, 0:64].rearrange("p (t n) -> p t n", t=NT), br, ALU.add), dve)
            for t_ in range(NT):
                ins = dve.max(top8[:, t_, :], logit[:, t_, :])
            link(ins, dve)
            for t_ in range(NT):
                dve.tensor_scalar(st_[:, 4 + t_:5 + t_], top8[:, t_, 0:1], -1.0, None, ALU.mult).then_inc(s_lm, 1) if t_ else \
                    dve.tensor_scalar(st_[:, 4 + t_:5 + t_], top8[:, t_, 0:1], -1.0, None, ALU.mult)
            for k in range(2):
                dve.memset(eqs[k], 0.0)
            for t_ in range(NT):
                ins = dve.tensor_scalar(more[:, t_, :], logit[:, t_, :], top8[:, t_, TOP - 1:TOP], None, ALU.is_gt)
            link(ins, dve)
            for t_ in range(NT):
                dve.tensor_scalar(equal[:, t_, :], logit[:, t_, :], top8[:, t_, TOP - 1:TOP], None, ALU.is_equal)
                dve.tensor_scalar(eqs[0][:, t_, 16:48], logit[:, t_, :], top8[:, t_, TOP - 1:TOP], None, ALU.is_equal)
            link(dve.tensor_reduce(st_[:, 0:2], more, AX.X, ALU.add), dve)
            ins = dve.tensor_scalar(st_[:, 0:2], st_[:, 0:2], -1.0, float(TOP), ALU.mult, ALU.add)
            link(ins, dve)
            cur = 0
            for sh in (1, 2, 4, 8, 16):
                link(dve.tensor_tensor(eqs[1 - cur][:, :, 16:48], eqs[cur][:, :, 16:48], eqs[cur][:, :, 16 - sh:48 - sh], ALU.add), dve)
                cur = 1 - cur
            for t_ in range(NT):
                ins = dve.scalar_tensor_tensor(tmp[:, t_, :], eqs[cur][:, t_, 16:48], st_[:, t_:t_ + 1], equal[:, t_, :], ALU.is_le, ALU.mult)
            link(ins, dve)
            link(dve.tensor_tensor(chosen, tmp, more, ALU.add), dve)
            dve.memset(over[:, 60:61], 0.0).then_inc(s_gt, 1)
            dve.wait_ge(s_le, 2)
            link(dve.tensor_tensor(gates, gates, chosen, ALU.mult), dve)
            link(dve.tensor_reduce(st_[:, 8:10], gates, AX.X, ALU.add), dve)
            link(dve.reciprocal(st_[:, 10:12], st_[:, 8:10]), dve)
            for t_ in range(NT):
                ins = dve.tensor_scalar(gates[:, t_, :], gates[:, t_, :], st_[:, 10 + t_:11 + t_], None, ALU.mult)
            link(ins, dve)
            dve.memset(over[:, 60:61], 0.0).then_inc(s_gt, 1)
            dve.wait_ge(s_ps, 1)
            link(dve.tensor_scalar(tmp, bank[2][:, 0:64].rearrange("p (t n) -> p t n", t=NT), 1.0, None, ALU.add), dve)
            link(dve.tensor_tensor(tmp, tmp, chosen, ALU.mult), dve)
            link(dve.tensor_scalar(posm, tmp, -1.0, None, ALU.add), dve)
            dve.tensor_scalar(over[0:E, 0:2], bank[3][0:E, 0:2], float(CAP), None, ALU.is_gt).then_inc(s_il, 1)
            dve.wait_ge(s_ps, 2)
            link(dve.tensor_copy(over[0:E, 4:5], bank[1][0:E, 0:1]), dve)
            dve.tensor_scalar(over[0:E, 8:16], c("slot")[0:E, 0:8], over[0:E, 4:5], over[0:E, 0:1], ALU.is_equal, ALU.mult).then_inc(s_il, 1)
            dve.wait_ge(s_ps, 3)
            dve.tensor_scalar(items[0:1, 0:1], bank[1][0:1, 0:1], float(E), None, ALU.add)
            dve.tensor_copy(items[0:1, 1:1 + E], c("slot")[0:1, 0:E])
            dve.tensor_copy(items[0:1, 1 + E:1 + ITEMS], bank[3][0:1, 0:8])
            dve.memset(items[0:1, 1 + ITEMS:1 + ITEMS + E], 0)
            link(dve.memset(items[0:1, 1 + ITEMS + E:1 + 2 * ITEMS], CAP), dve)
            dve.memset(over[:, 60:61], 0.0).then_inc(s_items, 1)
            dve.sem_inc(m_hid, 2)
            dve.sem_inc(m_add, 1)
            dve.wait_ge(s_items, 1)
            n = dve.value_load(items[0:1, 0:1], min_val=E, max_val=ITEMS - 1)

            def select(i, first=False):
                if first:
                    e, r0 = 0, 0
                else:
                    e = dve.value_load(items[0:1, bass.ds(i + 1, 1)], min_val=0, max_val=E - 1)
                    r0 = dve.value_load(items[0:1, bass.ds(i + 1 + ITEMS, 1)], min_val=0, max_val=CAP)
                for t_ in range(NT):
                    pc = posm[:, t_, 0:1] if first else big[:, bass.ds(40 * 256 + 5 * 64 + t_ * 32 + e, 1)]
                    gc = gates[:, t_, 0:1] if first else big[:, bass.ds(40 * 256 + 64 + t_ * 32 + e, 1)]
                    rows = c("slot")[:, 0:CAP] if first else con[:, bass.ds(CONST["slot"][0] + r0, CAP)]
                    dve.tensor_scalar(sel[:, t_, :], rows, pc, None, ALU.is_equal)
                    ins = dve.tensor_scalar(selw[:, t_, :], rows, pc, gc, ALU.is_equal, ALU.mult)
                ins.then_inc(m_sel, 1)
            select(0, True)
            steps = 2 * KB
            with dve.Fori(0, n) as i:
                e = dve.value_load(items[0:1, bass.ds(i + 1, 1)], min_val=0, max_val=E - 1)
                for j in range(KB):
                    bk = bank[4 + j % 2]
                    dve.wait_ge(moe_done, R + j + 1 + i * PER)
                    bg = bgu_s[:, bass.ds(e * 16 + j, 1)]
                    bu = bgu_s[:, bass.ds(e * 16 + KB + j, 1)]
                    dve.tensor_scalar(g1[:, j % 2, :], bk[:, 0:CAP], bg, LIMIT, ALU.add, ALU.min).then_inc(m_g1, 1)
                    dve.tensor_scalar(u1[:, j % 2, :], bk[:, CAP:2 * CAP], bu, LIMIT, ALU.add, ALU.min).then_inc(m_link, 1)
                    dve.wait_ge(m_link, 3 * j + 1 + i * 3 * KB)
                    dve.tensor_scalar(u1[:, j % 2, :], u1[:, j % 2, :], -LIMIT, 1.0, ALU.max, ALU.add).then_inc(m_link, 1)
                    dve.wait_ge(m_sig, j + 1 + i * KB)
                    dve.tensor_tensor(gs[:, j % 2, :], g1[:, j % 2, :], sg[:, j % 2, :], ALU.mult).then_inc(m_link, 1)
                    dve.wait_ge(m_link, 3 * j + 3 + i * 3 * KB)
                    dve.tensor_tensor(mh[:, j, :], gs[:, j % 2, :], u1[:, j % 2, :], ALU.mult).then_inc(m_hid, 1)
                select(i + 1)
                dve.wait_ge(m_scat, i + 1)
                for b_ in range(4):
                    o = xt[:, 2 * b_:2 * b_ + 2, :]
                    ins = dve.tensor_tensor(o, o, bank[(2, 3, 6, 7)[b_]][:, :].rearrange("p (a n) -> p a n", a=2), ALU.add)
                ins.then_inc(m_add, 1)
                dve.wait_ge(m_add, i + 2)
            dve.memset(over[:, 60:61], 0.0).then_inc(s_bd, 1)
            dve.wait_ge(moe_over, 1)
            for b_ in range(4):
                o = xt[:, 2 * b_:2 * b_ + 2, :]
                dve.tensor_tensor(o, o, bank[(2, 3, 6, 7)[b_]][:, :].rearrange("p (a n) -> p a n", a=2), ALU.add).then_inc(s_big, 1)
        stage(pe=moe_pe, act=moe_act, dve=moe_dve, sp=moe_sp)
        moe_stage = lambda eng, k: eng.wait_ge(s_big, k // 2 + 1)
        n_fin = norm_stage("first_final", xts, xts, ("norm_final", 0), D, eps1, moe_stage, none)

        src_wait = lambda eng, k: norm_ready(eng, n_fin, k)
        sl = dict(sq=sem("subln_squared"), sm=sem("subln_summed"), rt=sem("subln_root"), rd=sem("subln_ready"))
        sl_n = [0]
        for l in range(4):
            n_a = norm_stage(f"attn{l}", xts, hts, ("attn", 8 * l), D, eps2, src_wait, none)
            a_ready = lambda pe, n_a=n_a: norm_ready(pe, n_a)
            if l in (0, 3):
                lam = 0 if l == 0 else 1
                spec = [("T", True, 2 * i) for i in range(8)] + [("N", False, (16, i)) for i in range(4)]
                t = rope_stage(f"a_qkv{l}", POST_PH, post, POST["a_qkv", l], [(*x_, 0) for x_ in spec], hts, a_ready, c("rot_ac"), c("cs_ac"))
                va = area(16, 8).rearrange("p (t n) -> p t n", t=NT)
                oa = [area(24 + h, 1) for h in range(8)]
                o_n = attention(f"a{l}", 8, 1, 2,
                                lambda h, j, t_: [area(h, 1)[64 * j:64 * j + 64, t_ * P:(t_ + 1) * P]],
                                lambda h, j: [area(8 + h, 1)[64 * j:64 * j + 64, :]],
                                lambda h, ch, part: va[:, ch, h * P:(h + 1) * P], "one",
                                lambda n: oa[n], 64 ** -0.5, lambda pe, t=t: pe.wait_ge(s_evac, t), coef=lam_neg[:, lam:lam + 1])

                def sub_act(act, k=sl_n[0], o_n=o_n):
                    for h in range(8):
                        act.wait_ge(s_o, o_n - 8 + h + 1)
                        act.activation(sq[:, h, :], oa[h], ACT.Square).then_inc(sl["sq"], 1)
                    for b in range(4):
                        act.wait_ge(sl["sm"], 4 * k + b + 1)
                        act.activation(area(32 + 2 * b, 2), bank[b][:, :], ACT.Sqrt, bias=eps2[:, 0:1], scale=1.0 / P).then_inc(sl["rt"], 1)

                def sub_pe(pe, k=sl_n[0], o_n=o_n):
                    pe.wait_ge(s_o, o_n)
                    for h in range(8):
                        pe.wait_ge(sl["sq"], 8 * k + h + 1)
                        mm = pe.matmul(bank[h // 2][:, (h % 2) * S:(h % 2 + 1) * S], ones, sq[:, h, :], start=True, stop=True)
                        if h % 2:
                            mm.then_inc(sl["sm"], 1)

                def sub_dve(dve, k=sl_n[0], lam=lam):
                    for b in range(4):
                        dve.wait_ge(sl["rt"], 4 * k + b + 1)
                        link(dve.reciprocal(area(32 + 2 * b, 2), area(32 + 2 * b, 2)), dve)
                        for h in (2 * b, 2 * b + 1):
                            dve.scalar_tensor_tensor(hts[h], oa[h], sub_g[:, lam:lam + 1], area(32 + h, 1), ALU.mult, ALU.mult).then_inc(sl["rd"], 1)
                sl_n[0] += 1
                stage(act=sub_act, pe=sub_pe, dve=sub_dve)
                t = resid_stage(f"a_o{l}", POST_PH, post, POST["a_o", l], hts, lambda pe, n=sl_n[0]: pe.wait_ge(sl["rd"], 8 * n))
            elif l == 1:
                t = copy_stage("b_a", POST_PH, post, POST["b_a", l], "TTT", hts, a_ready, [blocks(area(2 * i, 2)) for i in range(3)])
                lat = lambda eng, k, t=t: eng.wait_ge(s_evac, t)
                s_kr, s_krd = sem("k_rope_rotated"), sem("k_rope_ready")

                def kr_pe(pe, t=t):
                    pe.wait_ge(s_evac, t)
                    pe.matmul(bank[1][:, 0:S], c("rot_b"), area(5, 1), start=True, stop=True).then_inc(s_kr, 1)

                def kr_dve(dve):
                    dve.wait_ge(s_kr, 1)
                    dve.tensor_tensor(m1[:, 0:S], area(5, 1), c("cs_b")[:, 0:S], ALU.mult)
                    link(dve.tensor_tensor(m2[:, 0:S], bank[1][:, 0:S], c("cs_b")[:, 512:512 + S], ALU.mult), dve)
                    dve.tensor_tensor(area(6, 1), m1[:, 0:S], m2[:, 0:S], ALU.add).then_inc(s_krd, 1)
                    dve.wait_ge(s_krd, 1)
                stage(pe=kr_pe, dve=kr_dve)
                n_q = norm_stage("b_q", [area(k, 1) for k in range(3)], [area(8 + k, 1) for k in range(3)], ("q_norm", 0), 384, eps2, lat, none)
                n_kv = norm_stage("b_kv", [area(3 + k, 1) for k in range(2)], [area(11 + k, 1) for k in range(2)], ("kv_norm", 0), 256, eps2, lat, none)
                spec = [("T", i >= 4, 16 + 2 * i, 0) for i in range(6)]
                rope_stage("b_qb", POST_PH, post, POST["b_q", l], spec, [area(8 + k, 1) for k in range(3)], lambda pe, n=n_q: norm_ready(pe, n), c("rot_b"), c("cs_b"), kc=3)
                kvs = [area(11 + k, 1) for k in range(2)]
                copy_stage("b_k", POST_PH, post, POST["b_k", l], "TTTT", kvs, lambda pe, n=n_kv: norm_ready(pe, n), [blocks(area(28 + 2 * i, 2)) for i in range(4)], kc=2)
                vb = area(36, 8).rearrange("p (t n) -> p t n", t=NT)
                t = copy_stage("b_v", POST_PH, post, POST["b_v", l], "NNNN", kvs, none, [vb[:, :, i * 256:(i + 1) * 256] for i in range(4)], kc=2)
                quad = [0, 2, 1, 3]
                o_n = attention("b", 16, 1, 1,
                                lambda h, j, t_: [area(16 + h // 2, 1)[64 * (h % 2):64 * (h % 2) + 64, t_ * P:(t_ + 1) * P],
                                                  area(24 + h // 4, 1)[32 * quad[h % 4]:32 * quad[h % 4] + 32, t_ * P:(t_ + 1) * P]],
                                lambda h, j: [area(28 + h // 2, 1)[64 * (h % 2):64 * (h % 2) + 64, :], area(6, 1)[32 * quad[h % 4]:32 * quad[h % 4] + 32, :]],
                                lambda h, ch, part: vb[:, ch, h * 64:h * 64 + 64], "half",
                                lambda n: hts[n], 96 ** -0.5, lambda pe, t=t: pe.wait_ge(s_evac, t))
                t = resid_stage("b_o", POST_PH, post, POST["b_o", l], hts, lambda pe, o_n=o_n: pe.wait_ge(s_o, o_n))
            else:
                spec = [("T", True, 2 * i, 0) for i in range(4)] + [("T", True, 24 + 2 * i, 0) for i in range(4)] + [("N", False, (48, i), 0) for i in range(4)]
                t = rope_stage("c_qkv", POST_PH, post, POST["c_qkv", l], spec, hts, a_ready, c("rot_ac"), c("cs_ac"), times=3, step=8)
                vc = [area(48 + 8 * j, 8).rearrange("p (t n) -> p t n", t=NT) for j in range(3)]
                masks = [c(f"mask{j}").rearrange("p (t n) -> p t n", t=NT) for j in range(3)]
                o_n = attention("c", 16, 3, 1,
                                lambda h, j, t_: [area(8 * j + h // 2, 1)[64 * (h % 2):64 * (h % 2) + 64, t_ * P:(t_ + 1) * P]],
                                lambda h, j: [area(24 + 8 * j + h // 2, 1)[64 * (h % 2):64 * (h % 2) + 64, :]],
                                lambda h, ch, part: vc[ch // 2][:, ch % 2, h * 64:h * 64 + 64], "half",
                                lambda n: hts[n], 64 ** -0.5, lambda pe, t=t: pe.wait_ge(s_evac, t), masks=masks)
                t = resid_stage("c_o", POST_PH, post, POST["c_o", l], hts, lambda pe, o_n=o_n: pe.wait_ge(s_o, o_n))
            n_f = norm_stage(f"ffn{l}", xts, hts, ("ffn", 8 * l), D, eps2, after_tiles(t), none)
            t = ffn_stage(l, lambda pe, n_f=n_f: norm_ready(pe, n_f))
            src_wait = after_tiles(t)
        n_last = norm_stage("last", xts, hts, ("final2", 0), D, eps2, src_wait, none)

        def last_sp(sp):
            norm_ready(sp, n_last)
            sp.dma_start(out, ht[:, :, :]).then_inc(s_out, 16)
            sp.wait_ge(s_out, 16)
        stage(sp=last_sp)

        @block.sync
        def _(sp):
            for st in STAGES:
                if st["sp"]:
                    st["sp"](sp)

        @block.tensor
        def _(pe):
            for st in STAGES:
                if st["pe"]:
                    st["pe"](pe)

        @block.scalar
        def _(act):
            for st in STAGES:
                if st["act"]:
                    st["act"](act)

        @block.vector
        def _(dve):
            for st in STAGES:
                if st["dve"]:
                    st["dve"](dve)


_PARAMS = ["x", "mem", "norm_mix", "w_in", "conv_w", "g_conv_out", "g_fft_out", "w_out", "norm_xattn", "norm_mem", "w_q",
           "w_k", "w_v", "w_o", "norm_ffn", "w_router", "b_router", "w_gate_up", "b_gate_up", "w_down", "b_down",
           "norm_final"]


def lay_out(inputs):
    a = {k: np.asarray(v) for k, v in inputs.items()}

    def channels(v):
        return np.ascontiguousarray(v.reshape(S, KB, P).transpose(2, 1, 0))

    def col(v):
        return v.reshape(-1, P).T

    def rep(v):
        return np.broadcast_to(v.reshape(1, -1), (P, v.size))

    def units(w, names=None):
        K, N = w.shape
        u = w.reshape(K // P, P, N // 256, 256).transpose(2, 1, 0, 3).reshape(N // 256, P, -1)
        out = np.zeros((u.shape[0], P, UW), np.float32)
        out[:, :, :u.shape[2]] = u
        return list(out)

    pre = []
    for n in ("w_in", "w_k", "w_v", "w_out", "w_q", "w_o"):
        pre += units(a[n][0])

    def gate_up(w, f):
        return w.reshape(KB, P, 2, f // P, P).transpose(3, 1, 0, 2, 4).reshape(f // P, P, UW)

    def rows(w):
        return w.reshape(-1, 2, P, D).transpose(0, 2, 1, 3).reshape(-1, P, UW)

    post = []
    for l in range(4):
        if l in (0, 3):
            post += units(a["a_w_qkv_2"][l // 3]) + units(a["a_w_o_2"][l // 3])
        elif l == 1:
            w = a["b_w_a_2"][0]
            post += units(np.concatenate([w[:, :640], w[:, 640:], w[:, 640:], w[:, 640:], w[:, 640:]], 1))
            q = a["b_w_qb_2"][0].reshape(384, 16, 96)
            order = [4 * b + o for b in range(4) for o in (0, 2, 1, 3)]
            post += units(np.concatenate([q[:, :, :64].reshape(384, 1024), q[:, order, 64:].reshape(384, 512)], 1))
            kv = a["b_w_kvb_2"][0].reshape(256, 16, 128)
            post += units(kv[:, :, :64].reshape(256, 1024)) + units(kv[:, :, 64:].reshape(256, 1024))
            post += units(a["b_w_o_2"][0])
        else:
            post += units(a["c_w_qkv_2"][0]) + units(a["c_w_o_2"][0])
        gu, dn = gate_up(a["f_w_gu_2"][l], FB * P), rows(a["f_w_out_2"][l])
        post += [gu[0], gu[1]]
        for j in range(1, FB // 2):
            post += [gu[2 * j], gu[2 * j + 1], dn[j - 1]]
        post.append(dn[FB // 2 - 1])
    lam = np.concatenate([a[f"a_lambda_{n}_2"][l] for l in range(2) for n in ("q1", "k1", "q2", "k2")])
    params = np.concatenate([
        col(a["norm_mix"][0]), col(a["norm_mem"][0]), col(a["norm_xattn"][0]), col(a["norm_ffn"][0]), col(a["norm_final"]),
        col(a["g_conv_out"][0]), col(a["g_fft_out"][0]), col(a["conv_w"][0].reshape(-1)), col(a["attn_norm_2"].reshape(-1)),
        col(a["ffn_norm_2"].reshape(-1)), col(a["final_norm_2"]), col(a["b_q_norm_2"].reshape(-1)), col(a["b_kv_norm_2"].reshape(-1)),
        col(a["a_subln_2"].reshape(-1)), rep(np.concatenate([a["b_router"][0]] * 2)), rep(lam)], 1)
    return {
        "xin": channels(a["x"][0]), "memin": channels(a["mem"][0]), "consts": CONSTS, "params": params,
        "pre": np.stack(pre), "post": np.stack(post),
        "router": a["w_router"][0].reshape(KB, P, E).transpose(1, 0, 2).reshape(P, -1),
        "bgu": a["b_gate_up"][0].reshape(E, 2 * KB, P).transpose(2, 0, 1).reshape(P, -1),
        "bdown": a["b_down"][0],
        "wgu": a["w_gate_up"][0].reshape(E, KB, P, 2, KB, P).transpose(0, 4, 2, 1, 3, 5).reshape(E, KB, P, UW),
        "wdn": a["w_down"][0].reshape(E, 4, 2, P, D).transpose(0, 1, 3, 2, 4).reshape(E, 4, P, UW),
    }


def kernel(**inputs):
    import concourse.bacc as bacc
    from concourse.bass_utils import run_bass_kernel_spmd
    arrays = {n: np.ascontiguousarray(v) for n, v in lay_out(inputs).items()}
    nc = bacc.Bacc("TRN2", target_bir_lowering=False, num_devices=1)
    aps = {n: nc.dram_tensor(n, v.shape, F32, kind="ExternalInput").ap() for n, v in arrays.items()}
    out = nc.dram_tensor("out", (P, KB, S), F32, kind="ExternalOutput").ap()
    program(nc, aps["xin"], aps["memin"], aps["consts"], aps["params"], aps["pre"], aps["post"],
            aps["router"], aps["bgu"], aps["bdown"], aps["wgu"], aps["wdn"], out)
    r = run_bass_kernel_spmd(nc, [arrays], core_ids=[0])
    got = r.results[0]["out"]
    return np.ascontiguousarray(got.transpose(2, 1, 0)).reshape(1, S, D)
```

```python
import math
import numpy as np
import concourse.bass as bass
from concourse import mybir
from contextlib import ExitStack

F32 = mybir.dt.float32
F32R = mybir.dt.float32r
I32 = mybir.dt.int32
ALU = mybir.AluOpType
ACT = mybir.ActivationFunctionType
AX = mybir.AxisListType

D = 1024
S = 256
P = 128
KB = D // P
NT = S // P
HALF = D // 2
CB = HALF // P
GROUP = 64
E = 32
TOP = 4
CAP = P
ITEMS = E + 8
FB = 22
EPS1, EPS2 = 1e-5, 1e-6
LIMIT, ALPHA = 7.0, 1.702
R = 4
SR = 2
UW = 2048
MASKED = -1e30

CONST = {}


def const_table():
    cols = []

    def put(name, a):
        a = np.asarray(a, np.float64).reshape(P, -1)
        CONST[name] = (sum(c.shape[1] for c in cols), a.shape[1])
        cols.append(a)

    put("ones", np.ones((P, P)))
    put("ident", np.eye(P))
    put("before", np.triu(np.ones((P, P)), 1))
    put("slot", np.tile(np.arange(2 * P), (P, 1)))
    put("expert", np.arange(P)[:, None])
    put("mod32", np.arange(P)[:, None] % E == np.arange(E)[None, :])
    put("rot_ac", rotation(64, 0, 8))
    put("cs_ac", rope_table(64, 0, 8))
    put("rot_b", rotation(32, 0, 16))
    put("cs_b", rope_table(32, 0, 16))
    q, k = np.arange(S)[:, None], np.arange(S)[None, :]
    near = np.abs(q - k) <= 64
    for name, ok in (("mask0", near), ("mask1", (q - k) % 4 == 0), ("mask2", (q - k) % 16 == 0)):
        m = np.where(ok, 0.0, MASKED * 8.0)
        put(name, m.reshape(NT, P, S).transpose(1, 0, 2) if name == "mask0" else m[0:P])
    return np.concatenate(cols, 1).astype(np.float32)


def dft_table():
    t = np.arange(S)
    ang = 2 * np.pi * ((t[:, None] * t[None, :]) % S) / S
    cs = np.concatenate([np.cos(ang), np.sin(ang)], 1) / math.sqrt(S)
    seq = cs.reshape(NT, P, 2 * S).transpose(1, 0, 2).reshape(P, -1)
    c = np.arange(GROUP)
    ang = 2 * np.pi * ((c[:, None] * c[None, :]) % GROUP) / GROUP
    two = np.eye(P // GROUP)
    own = [np.kron(two, f) / math.sqrt(GROUP) for f in (np.cos(ang), -np.sin(ang))]
    return np.concatenate([seq, *own], 1).astype(np.float32)


def rotation(head, at, r):
    m = np.zeros((head, head))
    for i in range(r):
        m[at + r + i, at + i] = -1.0
        m[at + i, at + r + i] = 1.0
    return np.kron(np.eye(P // head), m)


def rope_table(head, at, r):
    pos = np.arange(S, dtype=np.float32)
    inv = (np.float32(500000.0) ** (-np.arange(0, 2 * r, 2, dtype=np.float32) / np.float32(2 * r))).astype(np.float32)
    ang = (pos[:, None] * inv[None, :]).astype(np.float32).astype(np.float64)
    c, s = np.ones((head, S)), np.zeros((head, S))
    c[at:at + r], c[at + r:at + 2 * r] = np.cos(ang).T, np.cos(ang).T
    s[at:at + r], s[at + r:at + 2 * r] = np.sin(ang).T, np.sin(ang).T
    c, s = np.tile(c, (P // head, 1)), np.tile(s, (P // head, 1))
    return np.concatenate([c, c, s, s], 1)


CONSTS = const_table()
DFT = dft_table()

PARAM_SIZES = [
    ("norm_mix", 8), ("norm_mem", 8), ("norm_xattn", 8), ("norm_ffn", 8), ("norm_final", 8),
    ("g_conv", 4), ("g_fft", 4), ("conv_w", 12), ("attn", 32), ("ffn", 32), ("final2", 8),
    ("q_norm", 3), ("kv_norm", 2), ("subln", 2), ("b_router", 64), ("lam", 8 * 64),
]
PARAM = {}
_at = 0
for _n, _w in PARAM_SIZES:
    PARAM[_n] = _at
    _at += _w
NPARAM = _at

PRE = {"w_in": 0, "w_k": 8, "w_v": 12, "w_out": 16, "w_q": 20, "w_o": 24}
N_PRE = 28
POST = {}
_at = 0
LAYER_UNITS = {"a_qkv": 12, "a_o": 4, "b_a": 3, "b_q": 6, "b_k": 4, "b_v": 4, "b_o": 4, "c_qkv": 36, "c_o": 4}
LAYERS = [["a_qkv", "a_o"], ["b_a", "b_q", "b_k", "b_v", "b_o"], ["c_qkv", "c_o"], ["a_qkv", "a_o"]]
FFN_UNITS = FB + FB // 2
for _l, _names in enumerate(LAYERS):
    for _n in _names:
        POST[_n, _l] = _at
        _at += LAYER_UNITS[_n]
    POST["ffn", _l] = _at
    _at += FFN_UNITS
N_POST = _at


def program(nc, x, mem, consts, dft, params, pre, post, router, bgu, bdown, wgu, wdn, out):
    ctx = ExitStack()
    with ctx:
        def sb(name, shape, dt=F32):
            return ctx.enter_context(nc.sbuf_tensor(name, shape, dt))

        def sem(name):
            return ctx.enter_context(nc.semaphore(name))

        xt = sb("xt", [P, KB, S])
        ht = sb("ht_hi", [P, KB, S], F32R)
        hl = sb("ht_lo", [P, KB, S], F32R)
        hid_hi = sb("hid_hi", [P, 4, S], F32R)
        hid_lo = sb("hid_lo", [P, 4, S], F32R)
        w_hi = sb("w_hi", [P, SR, UW], F32R)
        w_lo = sb("w_lo", [P, SR, UW], F32R)
        ring = sb("ring", [P, R, UW])
        con = sb("con", [P, CONSTS.shape[1]])
        par = sb("par", [P, NPARAM])
        big_at = -(-nc.sbuf_base // 32) * 32
        big = sb("big", [P, 9 * 2048])
        prob = sb("prob", [P, 2, 1536])
        probt = sb("probt", [P, 1536])
        sq = prob[:, :, :].rearrange("p a n -> p (a n)")[:, 0:KB * S].rearrange("p (k n) -> p k n", n=S)
        root = sb("root", [P, S])
        rstd = sb("rstd", [P, S])
        eps1 = sb("eps1", [P, 1])
        eps2 = sb("eps2", [P, 1])
        small = sb("small", [P, 64])
        items = sb("items", [1, 1 + 2 * ITEMS], I32)
        bank = [ctx.enter_context(nc.psum_tensor(f"bank{b}", [P, 512], F32)) for b in range(8)]

        def c(name):
            a, n = CONST[name]
            return con[:, a:a + n]

        def g(name, k=0):
            return par[:, PARAM[name] + k:PARAM[name] + k + 1]

        def blocks(a, w=S):
            return a.rearrange("p (b n) -> p b n", n=w)

        def f32(a):
            return a.bitcast(F32)

        def area(at, n):
            return big[:, at * 256:(at + n) * 256]

        ones, ident = c("ones"), c("ident")

        s_x, s_mem, s_const = sem("x_loaded"), sem("mem_loaded"), sem("const_loaded")
        s_eps = sem("eps_set")
        pre_in = [sem(f"pre_in{i}") for i in range(R)]
        pre_done, pre_hi, pre_lo = sem("pre_unit_done"), sem("pre_unit_rounded"), sem("pre_unit_split")
        moe_in = [sem(f"moe_in{i}") for i in range(R)]
        moe_done = sem("moe_unit_done")
        moe_over = sem("moe_over")
        post_in = [sem(f"post_in{i}") for i in range(R)]
        post_done, post_hi, post_lo = sem("post_unit_done"), sem("post_unit_rounded"), sem("post_unit_split")
        s_nhi, s_nlo = sem("norm_rounded"), sem("norm_split")
        s_osp = sem("att_out_rounded")
        s_evac = sem("tile_evacuated")
        s_xadd = sem("residual_added")
        s_sq, s_sum, s_root, s_rstd, s_norm = (sem(n) for n in ("norm_squared", "norm_summed", "norm_root", "norm_rstd", "norm_ready"))
        s_link = sem("dve_step")
        s_raw, s_rot = sem("rope_raw"), sem("rope_rotated")
        s_fpq, s_fpe, s_fy = sem("fft_seq_done"), sem("fft_seq_copied"), sem("fft_group_done")
        s_sc, s_max, s_exp, s_prob, s_tr, s_pt, s_pv, s_o = (sem("att_" + n) for n in ("scores", "max", "exp", "prob", "turned", "probt", "pv", "out"))
        s_sig = sem("ffn_sigmoid")
        s_out = sem("out_written")

        block = ctx.enter_context(nc.Block())

        class Phase:

            def __init__(self, arrived, hi, lo, done, n):
                self.arrived, self.hi, self.lo, self.done, self.n = arrived, hi, lo, done, n
                self.width = {}

            def cols(self, u):
                return self.width.get(u, UW)

        PRE_PH = Phase(pre_in, pre_hi, pre_lo, pre_done, N_PRE)
        POST_PH = Phase(post_in, post_hi, post_lo, post_done, N_POST)
        for l_, names_ in enumerate(LAYERS):
            for n_ in names_:
                kc_ = {"b_q": 3, "b_k": 2, "b_v": 2}.get(n_, KB)
                for u_ in range(LAYER_UNITS[n_]):
                    POST_PH.width[POST[n_, l_] + u_] = kc_ * 256

        def split_act(act, ph, u, i=0, per=0):
            if u >= ph.n:
                return
            w = ph.cols(u)
            act.wait_ge(ph.arrived[u % R], 16 * (u // R + 1) + i * (16 * per // R))
            if u >= SR:
                act.wait_ge(ph.done, u - SR + 1 + i * per)
            act.activation(w_hi[:, u % SR, 0:w], ring[:, u % R, 0:w], ACT.Copy).then_inc(ph.hi, 1)

        def split_dve(dve, ph, u, i=0, per=0):
            if u >= ph.n:
                return
            w = ph.cols(u)
            dve.wait_ge(ph.hi, u + 1 + i * per)
            dve.tensor_tensor(w_lo[:, u % SR, 0:w], ring[:, u % R, 0:w], f32(w_hi[:, u % SR, 0:w]), ALU.subtract).then_inc(ph.lo, 1)

        def wait_unit(pe, ph, u, i=0, per=0):
            pe.wait_ge(ph.lo, u + 1 + i * per)

        def products(pe, out, w, x, k0, k1, start, stop, **kw):
            for k in range(k0, k1):
                (wh, wl), (xh, xl) = w(k), x(k)
                pe.matmul(out, wh, xh, start=start and k == k0, stop=False, **kw)
                pe.matmul(out, wh, xl, start=False, stop=False, **kw)
                mm = pe.matmul(out, wl, xh, start=False, stop=stop and k == k1 - 1, **kw)
            return mm

        def slot(u, k):
            return ring[:, u % R, :].rearrange("p (k n) -> p k n", k=k)

        NORMS, norm_base = [], []

        def add_norm(name, src, dst, gain, n, eps, src_wait, dst_wait):
            norm_base.append(sum(len(j["src"]) for j in NORMS))
            lo = None
            if isinstance(dst, tuple):
                dst, lo = dst
            split_base = sum(len(j["src"]) for j in NORMS if j["lo"] is not None)
            NORMS.append(dict(name=name, src=src, dst=dst, lo=lo, split_base=split_base, gain=gain, n=n, eps=eps, src_wait=src_wait, dst_wait=dst_wait))
            return len(NORMS) - 1

        def norm_ready(eng, j, k=None):
            n = len(NORMS[j]["src"]) if k is None else k + 1
            if NORMS[j]["lo"] is not None:
                eng.wait_ge(s_nlo, NORMS[j]["split_base"] + n)
            else:
                eng.wait_ge(s_norm, norm_base[j] + n)

        def norm_act(act, j):
            m = NORMS[j]
            if j >= 1:
                act.wait_ge(s_sum, j)
            if m["split_base"]:
                act.wait_ge(s_nlo, m["split_base"])
            for k, a in enumerate(m["src"]):
                m["src_wait"](act, k)
                act.activation(sq[:, k, :], a, ACT.Square).then_inc(s_sq, 1)
            act.wait_ge(s_sum, j + 1)
            if j >= 1:
                act.wait_ge(s_rstd, j)
            act.activation(root[:, :], bank[0][:, 0:S], ACT.Sqrt, bias=m["eps"][:, 0:1], scale=1.0 / m["n"]).then_inc(s_root, 1)
            if m["lo"] is not None:
                for k in range(len(m["src"])):
                    act.wait_ge(s_norm, norm_base[j] + k + 1)
                    act.activation(m["dst"][k], sq[:, k, :], ACT.Copy).then_inc(s_nhi, 1)

        def norm_pe(pe, j):
            m = NORMS[j]
            if j >= 1:
                pe.wait_ge(s_root, j)
            for k in range(len(m["src"])):
                pe.wait_ge(s_sq, norm_base[j] + k + 1)
                mm = pe.matmul(bank[0][:, 0:S], ones, sq[:, k, :], start=(k == 0), stop=(k == len(m["src"]) - 1))
            mm.then_inc(s_sum, 1)

        def norm_dve(dve, j):
            m = NORMS[j]
            if j >= 1:
                dve.wait_ge(s_norm, norm_base[j])
            split = m["lo"] is not None
            out = [sq[:, k, :] for k in range(len(m["src"]))] if split else m["dst"]
            dve.wait_ge(s_root, j + 1)
            dve.reciprocal(rstd[:, :], root[:, :]).then_inc(s_rstd, 1)
            dve.wait_ge(s_rstd, j + 1)
            m["dst_wait"](dve)
            for k, a in enumerate(m["src"]):
                m["src_wait"](dve, k)
                dve.scalar_tensor_tensor(out[k], a, g(m["gain"][0], m["gain"][1] + k), rstd[:, :], ALU.mult, ALU.mult).then_inc(s_norm, 1)
            if split:
                for k in range(len(m["src"])):
                    dve.wait_ge(s_nhi, m["split_base"] + k + 1)
                    dve.tensor_tensor(m["lo"][k], out[k], f32(m["dst"][k]), ALU.subtract).then_inc(s_nlo, 1)

        class Link:
            n = 0

            def __call__(self, ins, dve):
                ins.then_inc(s_link, 1)
                self.n += 1
                dve.wait_ge(s_link, self.n)

        link = Link()

        JOBS = {}
        tiles_so_far = [0]

        def add_tiles(name, n):
            JOBS[name] = tiles_so_far[0]
            tiles_so_far[0] += n
            return JOBS[name]

        def tile_bank(t):
            return bank[4 + t % 4]

        def tile_free(pe, t, i=0, per=0):
            if t >= 4:
                pe.wait_ge(s_evac, t - 3 + i * per)

        def project(pe, ph, u, t, kind, src, kc=KB, i=0, per=0, tper=None):
            wait_unit(pe, ph, u, i, per)
            tile_free(pe, t, i, per if tper is None else tper)
            wh, wl = (w_[:, u % SR, 0:kc * 256].rearrange("p (k n) -> p k n", k=kc) for w_ in (w_hi, w_lo))
            o = tile_bank(t)
            for h in range(2):
                if kind == "T":
                    mm = products(pe, o[:, h * S:(h + 1) * S], lambda k: (wh[:, k, h * P:(h + 1) * P], wl[:, k, h * P:(h + 1) * P]), lambda k: src[k], 0, kc, True, True)
                else:
                    mm = products(pe, o[:, h * S:(h + 1) * S], lambda k: (src[k][0][:, h * P:(h + 1) * P], src[k][1][:, h * P:(h + 1) * P]), lambda k: (wh[:, k, :], wl[:, k, :]), 0, kc, True, True)
            mm.then_inc(ph.done, 1)

        def tile_done(eng, ph, u, i=0, per=0):
            eng.wait_ge(ph.done, u + 1 + i * per)

        his = [ht[:, k, :] for k in range(KB)]
        los = [hl[:, k, :] for k in range(KB)]
        hts = list(zip(his, los))
        xts = [xt[:, k, :] for k in range(KB)]

        z = [area(k, 1) for k in range(12)]
        u_tok = area(12, 4).rearrange("p (t n) -> p t n", t=NT)
        pq = area(16, 8).rearrange("p (b n) -> p b n", n=2 * S)
        yf = [area(24 + k, 1) for k in range(CB)]
        yc = [area(28 + k, 1) for k in range(CB)]
        cv = big[:, 32 * 256:32 * 256 + CB * (S + 2)].rearrange("p (b n) -> p b n", n=S + 2)
        dft_s = area(64, 5)
        dft_seq = dft_s[:, 0:1024].rearrange("p (t n) -> p t n", t=NT)
        mt = [area(40 + k, 1) for k in range(KB)]
        kx = [area(48 + k, 1) for k in range(KB)]
        vx = area(56, 8).rearrange("p (t n) -> p t n", t=NT)
        qx = [area(64 + k, 1) for k in range(KB)]
        memt = blocks(area(40, 8))
        raw = probt[:, 0:1024].rearrange("p (a n) -> p a n", a=2)
        m1 = prob[:, 0, 0:512]
        m2 = prob[:, 0, 512:1024]

        xadds = [0]
        STAGES = []

        def stage(pe=None, act=None, dve=None, sp=None):
            STAGES.append(dict(pe=pe, act=act, dve=dve, sp=sp))

        def loads(ph, dram, u0, n, width=UW):
            def run(sp):
                for u in range(u0, u0 + n):
                    if u >= R:
                        sp.wait_ge(ph.lo, u - R + 1)
                    elif ph is POST_PH and u == 0:
                        sp.wait_ge(moe_over, 1)
                    sp.dma_start(ring[:, u % R, 0:width], dram[u, :, 0:width]).then_inc(ph.arrived[u % R], 16)
            return run

        def splits_act(ph, u0, n):
            def run(act):
                for u in range(u0, u0 + n):
                    split_act(act, ph, u + SR)
            return run

        def copy_stage(name, ph, dram, u0, kinds, src, src_ready, dests, kc=KB):
            n = len(kinds)
            t0 = add_tiles(name, n)

            def pe_(pe):
                src_ready(pe)
                for i in range(n):
                    project(pe, ph, u0 + i, t0 + i, kinds[i], src, kc)

            def dve_(dve):
                for i in range(n):
                    split_dve(dve, ph, u0 + i + SR)
                    tile_done(dve, ph, u0 + i)
                    dve.tensor_copy(dests[i], tile_bank(t0 + i)[:, :].rearrange("p (a n) -> p a n", a=2)).then_inc(s_evac, 1)
            stage(pe=pe_, dve=dve_, act=splits_act(ph, u0, n), sp=loads(ph, dram, u0, n, kc * 256))
            return t0 + n

        def resid_stage(name, ph, dram, u0, src, src_ready):
            t0 = add_tiles(name, 4)
            x0 = xadds[0]
            xadds[0] += 4

            def pe_(pe):
                src_ready(pe)
                for i in range(4):
                    project(pe, ph, u0 + i, t0 + i, "T", src)

            def dve_(dve):
                for i in range(4):
                    split_dve(dve, ph, u0 + i + SR)
                    tile_done(dve, ph, u0 + i)
                    if x0 == 0:
                        dve.wait_ge(s_x, 16)
                    o = xt[:, 2 * i:2 * i + 2, :]
                    dve.tensor_tensor(o, o, tile_bank(t0 + i)[:, :].rearrange("p (a n) -> p a n", a=2), ALU.add).then_inc(s_evac, 1)
            stage(pe=pe_, dve=dve_, act=splits_act(ph, u0, 4), sp=loads(ph, dram, u0, 4))
            return t0

        def norm_stage(*a, **k):
            j = add_norm(*a, **k)
            stage(pe=lambda pe: norm_pe(pe, j), act=lambda act: norm_act(act, j), dve=lambda dve: norm_dve(dve, j))
            return j

        def after_tiles(t0):
            return lambda eng, k: eng.wait_ge(s_evac, t0 + k // 2 + 1)

        def none(*a):
            pass

        osp = [0]
        att_count = dict(sc=0, mx=0, exp=0, prob=0, tr=0, pt=0, pv=0, o=0)

        def attention(name, heads, groups, twins, q, k, v, pv_parts, o_dst, scale, ready, masks=None, coef=None, o_free=None):
            base = dict(att_count)
            att_count["sc"] += heads
            att_count["mx"] += heads
            att_count["exp"] += heads
            att_count["prob"] += heads
            att_count["tr"] += heads
            att_count["pt"] += heads
            pairs = pv_parts == "half"
            att_count["pv"] += heads
            att_count["o"] += heads // 2 if pairs else heads
            nb = groups * twins
            W = groups * S

            def sbank(h, j):
                return bank[j] if nb > 1 else bank[h % 2]

            def tbank(h, j):
                return bank[3 + j] if groups > 1 else bank[3 + h % 2]

            def obank(h):
                n = h // 2 if pairs else h
                return bank[6 + n % 2]

            def scores(pe, h):
                if nb > 1 and h >= 1:
                    if masks:
                        pe.wait_ge(s_max, base["mx"] + h)
                    else:
                        pe.wait_ge(s_exp, base["exp"] + h)
                if nb == 1 and h >= 2:
                    pe.wait_ge(s_exp, base["exp"] + h - 1)
                for j in range(nb):
                    for t in range(NT):
                        parts = q(h, j, t)
                        rhs = k(h, j)
                        for a in range(len(parts)):
                            mm = pe.matmul(sbank(h, j)[:, t * S:(t + 1) * S], parts[a], rhs[a], start=(a == 0), stop=(a == len(parts) - 1))
                mm.then_inc(s_sc, 1)

            def pr(h, w=0):
                return prob[:, h % 2, w * 512:w * 512 + NT * W].rearrange("p (t n) -> p t n", t=NT)

            def turn(pe, h):
                pe.wait_ge(s_prob, base["prob"] + h + 1)
                if groups > 1 and h >= 1:
                    pe.wait_ge(s_pt, base["pt"] + h)
                if groups == 1 and h >= 2:
                    pe.wait_ge(s_pt, base["pt"] + h - 1)
                for ch in range(W // P):
                    for t in range(NT):
                        mm = pe.transpose(tbank(h, ch // 2)[:, (ch % 2) * S + t * P:(ch % 2) * S + (t + 1) * P],
                                          pr(h)[:, t, ch * P:(ch + 1) * P], ident)
                mm.then_inc(s_tr, 1)

            def times_v(pe, h):
                pe.wait_ge(s_pt, base["pt"] + h + 1)
                n = h // 2 if pairs else h
                if n >= 2 and not (pairs and h % 2):
                    pe.wait_ge(s_o, base["o"] + n - 1)
                pt = probt[:, 0:NT * W].rearrange("p (c n) -> p c n", n=S)
                for part in range(2 if pv_parts == "two" else 1):
                    for ch in range(W // P):
                        if pairs:
                            o = obank(h)[64 * (h % 2):64 * (h % 2) + 64, 0:S]
                        else:
                            o = obank(h)[:, part * S:(part + 1) * S]
                        mm = pe.matmul(o, v(h, ch, part), pt[:, ch, :], start=(ch == 0), stop=(ch == W // P - 1))
                mm.then_inc(s_pv, 1)

            def pe_(pe):
                ready(pe)
                scores(pe, 0)
                if heads > 1:
                    scores(pe, 1)
                for h in range(heads):
                    turn(pe, h)
                    if h + 2 < heads:
                        scores(pe, h + 2)
                    times_v(pe, h)

            sm = small

            def col(h, what, w=0):
                a = (h % 2) * 24 + {"max": 0, "sum": 8, "r": 16}[what] + 2 * w
                return a

            def maxes(dve, h):
                dve.wait_ge(s_sc, base["sc"] + h + 1)
                if h >= 2:
                    dve.wait_ge(s_tr, base["tr"] + h - 1)
                if masks:
                    for j in range(groups):
                        for t_ in range(NT):
                            m_ = masks[j][:, t_ * S:(t_ + 1) * S] if masks[j].shape[1] > S else masks[j]
                            mins = dve.tensor_tensor(pr(h)[:, t_, j * S:(j + 1) * S], bank[j][:, t_ * S:(t_ + 1) * S], m_, ALU.add)
                    link(mins, dve)
                    src = [pr(h)]
                else:
                    src = [sbank(h, w)[:, :].rearrange("p (t n) -> p t n", t=NT) for w in range(twins)]
                for w, a in enumerate(src):
                    m = col(h, "max", w)
                    mins = dve.tensor_reduce(sm[:, m:m + 2], a, AX.X, ALU.max)
                link(mins, dve)
                m = col(h, "max")
                dve.tensor_scalar(sm[:, m:m + 2 * twins], sm[:, m:m + 2 * twins], -scale, None, ALU.mult).then_inc(s_max, 1)

            def exps(act, h):
                act.wait_ge(s_max, base["mx"] + h + 1)
                if h >= 2:
                    act.wait_ge(s_prob, base["prob"] + h - 1)
                    act.wait_ge(s_tr, base["tr"] + h - 1)
                for w in range(twins):
                    for t in range(NT):
                        src = pr(h)[:, t, :] if masks else sbank(h, w)[:, t * S:(t + 1) * S]
                        m, s_ = col(h, "max", w) + t, col(h, "sum", w) + t
                        ins = act.activation(pr(h, w)[:, t, :], src, ACT.Exp, bias=sm[:, m:m + 1], scale=scale, accum_out=sm[:, s_:s_ + 1])
                ins.then_inc(s_exp, 1)

            def norms(dve, h):
                dve.wait_ge(s_exp, base["exp"] + h + 1)
                s_, r = col(h, "sum"), col(h, "r")
                link(dve.reciprocal(sm[:, r:r + 2 * twins], sm[:, s_:s_ + 2 * twins]), dve)
                if twins == 2:
                    link(dve.tensor_scalar(sm[:, r + 2:r + 4], sm[:, r + 2:r + 4], coef, None, ALU.mult), dve)
                    for t in range(NT):
                        ins = dve.tensor_scalar(pr(h, 1)[:, t, :], pr(h, 1)[:, t, :], sm[:, r + 2 + t:r + 3 + t], None, ALU.mult)
                    link(ins, dve)
                    for t in range(NT):
                        ins = dve.scalar_tensor_tensor(pr(h)[:, t, :], pr(h)[:, t, :], sm[:, r + t:r + t + 1], pr(h, 1)[:, t, :], ALU.mult, ALU.add)
                else:
                    for t in range(NT):
                        ins = dve.tensor_scalar(pr(h)[:, t, :], pr(h)[:, t, :], sm[:, r + t:r + t + 1], None, ALU.mult)
                ins.then_inc(s_prob, 1)

            def turned(act, h):
                act.wait_ge(s_tr, base["tr"] + h + 1)
                if h >= 1:
                    act.wait_ge(s_pv, base["pv"] + h)
                for j in range(groups):
                    ins = act.activation(probt[:, j * 512:(j + 1) * 512], tbank(h, j)[:, :], ACT.Copy)
                ins.then_inc(s_pt, 1)

            def outs(dve, n):
                if o_free is not None and n == 0:
                    o_free(dve)
                dve.wait_ge(s_pv, base["pv"] + (2 * n + 2 if pairs else n + 1))
                b = bank[6 + n % 2]
                if pv_parts == "two":
                    src = b[:, :].rearrange("p (a n) -> p a n", a=2)
                else:
                    src = b[:, 0:S]
                if isinstance(o_dst(n), tuple):
                    hi, lo = o_dst(n)
                    osp[0] += 1
                    dve.tensor_copy(hi, src).then_inc(s_osp, 1)
                    dve.wait_ge(s_osp, osp[0])
                    dve.tensor_tensor(lo, src, f32(hi), ALU.subtract).then_inc(s_o, 1)
                else:
                    dve.tensor_copy(o_dst(n), src).then_inc(s_o, 1)

            def dve_(dve):
                maxes(dve, 0)
                for h in range(heads):
                    if h + 1 < heads:
                        maxes(dve, h + 1)
                    norms(dve, h)
                    if h >= 1:
                        if not pairs:
                            outs(dve, h - 1)
                        elif h % 2 == 0:
                            outs(dve, h // 2 - 1)
                outs(dve, heads // 2 - 1 if pairs else heads - 1)

            def act_(act):
                exps(act, 0)
                for h in range(heads):
                    if h + 1 < heads:
                        exps(act, h + 1)
                    turned(act, h)
            stage(pe=pe_, act=act_, dve=dve_)
            return base["o"] + (heads // 2 if pairs else heads)


        rope_count = [0]

        def rope_stage(name, ph, dram, u0, spec, src, src_ready, rot, tabs, kc=KB, times=1, step=0):
            n = len(spec)
            t0 = add_tiles(name, n * times)
            r0 = rope_count[0]
            per_r = sum(1 for x_ in spec if x_[1])
            rope_count[0] += per_r * times
            R_ = rot
            cos2, sin2 = tabs[:, 0:512], tabs[:, 512:1024]

            def index(l):
                return sum(1 for x_ in spec[:l] if x_[1])

            turned_at = [l for l in range(n) if spec[l][1]]

            def wait_two_before(eng, l, i):
                a = index(l)
                if a >= 2:
                    eng.wait_ge(s_evac, t0 + turned_at[a - 2] + 1 + i * n)
                elif r0 or times > 1 or t0:
                    eng.wait_ge(s_evac, t0 + i * n)

            def place(l, i):
                kind, turned_, at, _ = spec[l]
                if kind == "T":
                    a = big[:, bass.ds(i * (step * 256) + at * 256, 512)] if times > 1 else big[:, at * 256:at * 256 + 512]
                    return a.rearrange("p (a n) -> p a n", a=2)
                m, o = at
                if times > 1:
                    a = big[:, bass.ds(i * (step * 256) + m * 256, 2048)]
                else:
                    a = big[:, m * 256:m * 256 + 2048]
                return a.rearrange("p (t n) -> p t n", t=NT)[:, :, o * 256:(o + 1) * 256]

            def rot_one(pe, l, i):
                r = r0 + index(l)
                pe.wait_ge(s_raw, r + 1 + i * per_r)
                wait_two_before(pe, l, i)
                pe.matmul(bank[1 + r % 2][:, :], R_, raw[:, r % 2, :], start=True, stop=True).then_inc(s_rot, 1)

            def body_pe(pe, i):
                for l in range(n):
                    project(pe, ph, u0 + l, t0 + l, spec[l][0], src, kc, i, n)
                    if l >= 1 and spec[l - 1][1]:
                        rot_one(pe, l - 1, i)
                if spec[n - 1][1]:
                    rot_one(pe, n - 1, i)

            def body_act(act, i):
                for l in range(n):
                    split_act(act, ph, u0 + l + SR, i, n)
                    if l not in turned_at:
                        continue
                    r = r0 + index(l)
                    tile_done(act, ph, u0 + l, i, n)
                    wait_two_before(act, l, i)
                    act.activation(raw[:, r % 2, :], tile_bank(t0 + l)[:, :], ACT.Copy).then_inc(s_raw, 1)

            def body_dve(dve, i, base, dyn):
                k = 0
                for l in range(n):
                    b2 = tile_bank(t0 + l)[:, :].rearrange("p (a n) -> p a n", a=2)
                    split_dve(dve, ph, u0 + l + SR, i, n)
                    if not spec[l][1]:
                        tile_done(dve, ph, u0 + l, i, n)
                        dve.tensor_copy(place(l, i), b2).then_inc(s_evac, 1)
                        continue
                    r = r0 + index(l)
                    dve.wait_ge(s_raw, r + 1 + i * per_r)
                    dve.wait_ge(s_evac, t0 + l + i * n)
                    dve.tensor_tensor(m1, raw[:, r % 2, :], cos2, ALU.mult)
                    dve.wait_ge(s_rot, r + 1 + i * per_r)
                    dve.tensor_tensor(m2, bank[1 + r % 2][:, :], sin2, ALU.mult).then_inc(s_link, 1)
                    k += 1
                    dve.wait_ge(s_link, base + k + dyn)
                    m1b, m2b = (m_.rearrange("p (a n) -> p a n", a=2) for m_ in (m1, m2))
                    dve.tensor_tensor(place(l, i), m1b, m2b, ALU.add).then_inc(s_evac, 1)

            def pe_(pe):
                src_ready(pe)
                if times == 1:
                    body_pe(pe, 0)
                else:
                    with pe.Fori(0, times) as i:
                        body_pe(pe, i)

            def act_(act):
                if times == 1:
                    body_act(act, 0)
                else:
                    with act.Fori(0, times) as i:
                        body_act(act, i)

            def dve_(dve):
                base = link.n
                if times == 1:
                    body_dve(dve, 0, base, 0)
                else:
                    with dve.Fori(0, times) as i:
                        body_dve(dve, i, base, i * per_r)
                link.n = base + per_r * times

            def sp_(sp):
                if times == 1:
                    return loads(ph, dram, u0, n, kc * 256)(sp)
                with sp.Fori(0, times) as i:
                    for l in range(n):
                        u = u0 + l
                        sp.wait_ge(ph.lo, u - R + 1 + i * n)
                        sp.dma_start(ring[:, u % R, :], dram[bass.ds(i * n + u, 1), :, :].rearrange("a p n -> (a p) n")).then_inc(ph.arrived[u % R], 16)
            stage(pe=pe_, act=act_, dve=dve_, sp=sp_)
            return t0 + n * times

        sgm = area(4, 2).rearrange("p (b n) -> p b n", n=S)
        gsg = area(6, 2).rearrange("p (b n) -> p b n", n=S)
        full = area(8, 2).rearrange("p (b n) -> p b n", n=S)
        sig_count = [0]

        def ffn_stage(l, src_ready):
            u0 = POST["ffn", l]
            t0 = add_tiles(("ffn", l), FB)
            g0 = sig_count[0]
            sig_count[0] += FB
            x0 = add_tiles(("ffn_x", l), 4)

            def gu(q):
                return u0 + (q if q < 2 else 2 + 3 * (q // 2 - 1) + q % 2)

            def ou(j):
                return u0 + 4 + 3 * j if j < FB // 2 - 1 else u0 + FFN_UNITS - 1

            JL = 4
            LOOPS = (FB // 2 - 3) // JL
            UP, TP = 3 * JL, 2 * JL

            def in_order(j):
                return [(gu(2 * j), 2 * j, None), (gu(2 * j + 1), 2 * j + 1, None)] + ([(ou(j - 1), None, j - 1)] if j else [])

            def out_unit(pe, j, i=0):
                u = ou(j)
                wait_unit(pe, POST_PH, u, i, UP)
                pe.wait_ge(s_evac, t0 + 2 * j + 2 + i * TP)
                wh, wl = (w_[:, u % SR, :].rearrange("p (k n) -> p k n", k=2) for w_ in (w_hi, w_lo))
                for k in range(2):
                    for d in range(KB):
                        hb = (2 * j + k) % 4
                        mm = products(pe, bank[d // 2][:, (d % 2) * S:(d % 2 + 1) * S], lambda k_: (wh[:, k_, d * P:(d + 1) * P], wl[:, k_, d * P:(d + 1) * P]),
                                      lambda k_: (hid_hi[:, hb, :], hid_lo[:, hb, :]), k, k + 1,
                                      j == 0 and k == 0 and d % 2 == 0, j == FB // 2 - 1 and k == 1, skip_group_check=True)
                mm.then_inc(post_done, 1)

            def step_pe(pe, j, i=0):
                for u, q, o in in_order(j):
                    if o is None:
                        project(pe, POST_PH, u, t0 + q, "T", hts, KB, i, UP, TP)
                    else:
                        out_unit(pe, o, i)

            def each(eng, step):
                for j in (0, 1):
                    step(eng, j, 0)
                with eng.Fori(0, LOOPS) as i:
                    for j in range(2, 2 + JL):
                        step(eng, j, i)
                step(eng, FB // 2 - 1, 0)

            def pe_(pe):
                src_ready(pe)
                each(pe, step_pe)
                out_unit(pe, FB // 2 - 1)

            def step_act(act, j, i):
                for u, q, o in in_order(j):
                    split_act(act, POST_PH, u + SR, i, UP)
                    if o is None:
                        act.wait_ge(post_done, u + 1 + i * UP)
                        if g0 + q >= 2:
                            act.wait_ge(s_evac, t0 + q - 1 + i * TP)
                        act.activation(sgm[:, q % 2, :], tile_bank(t0 + q)[:, 0:S], ACT.Sigmoid).then_inc(s_sig, 1)

            def act_(act):
                each(act, step_act)
                split_act(act, POST_PH, ou(FB // 2 - 1) + SR)

            def step_dve(dve, j, i, base):
                for u, q, o in in_order(j):
                    split_dve(dve, POST_PH, u + SR, i, UP)
                    if o is not None:
                        continue
                    k = base + 3 * q + i * (3 * TP)
                    dve.wait_ge(s_sig, g0 + q + 1 + i * TP)
                    dve.tensor_tensor(gsg[:, q % 2, :], tile_bank(t0 + q)[:, 0:S], sgm[:, q % 2, :], ALU.mult).then_inc(s_link, 1)
                    dve.wait_ge(s_link, k + 1)
                    if q >= 4:
                        dve.wait_ge(post_done, ou(q // 2 - 2) + 1 + i * UP)
                    up = tile_bank(t0 + q)[:, S:2 * S]
                    dve.tensor_tensor(hid_hi[:, q % 4, :], gsg[:, q % 2, :], up, ALU.mult)
                    dve.tensor_tensor(full[:, q % 2, :], gsg[:, q % 2, :], up, ALU.mult).then_inc(s_link, 2)
                    dve.wait_ge(s_link, k + 3)
                    dve.tensor_tensor(hid_lo[:, q % 4, :], full[:, q % 2, :], f32(hid_hi[:, q % 4, :]), ALU.subtract).then_inc(s_evac, 1)

            def dve_(dve):
                base = link.n
                each(dve, lambda d_, j, i: step_dve(d_, j, i, base))
                link.n = base + 3 * FB
                split_dve(dve, POST_PH, ou(FB // 2 - 1) + SR)
                dve.wait_ge(post_done, u0 + FFN_UNITS)
                for b in range(4):
                    o = xt[:, 2 * b:2 * b + 2, :]
                    dve.tensor_tensor(o, o, bank[b][:, :].rearrange("p (a n) -> p a n", a=2), ALU.add).then_inc(s_evac, 1)

            def sp_(sp):
                loads(POST_PH, post, u0, 5)(sp)
                with sp.Fori(0, LOOPS) as i:
                    for n_ in range(UP):
                        u = u0 + 5 + n_
                        sp.wait_ge(post_lo, u - R + 1 + i * UP)
                        sp.dma_start(ring[:, u % R, :], post[bass.ds(i * UP + u, 1), :, :].rearrange("a p n -> (a p) n")).then_inc(post_in[u % R], 16)
                loads(POST_PH, post, u0 + 29, 4)(sp)
            stage(pe=pe_, act=act_, dve=dve_, sp=sp_)
            return x0

        def first_sp(sp):
            sp.dma_start(xt[:, :, :], x).then_inc(s_x, 16)
            sp.dma_start(con[:, :], consts).then_inc(s_const, 16)
            sp.dma_start(par[:, :], params).then_inc(s_const, 16)
            sp.dma_start(dft_s, dft).then_inc(s_const, 16)
            sp.dma_start(memt, mem).then_inc(s_mem, 16)

        def first_dve(dve):
            dve.memset(eps1[:, :], EPS1).then_inc(s_eps, 1)
            dve.memset(eps2[:, :], EPS2).then_inc(s_eps, 1)
            dve.wait_ge(s_const, 48)

        def first_act(act):
            act.wait_ge(s_const, 48)
            act.wait_ge(s_eps, 2)
        stage(pe=lambda pe: pe.wait_ge(s_const, 48), act=first_act, dve=first_dve, sp=first_sp)

        lamw = sb("lamw", [P, 64])
        lam_e = sb("lam_e", [P, 8])
        lam_neg = sb("lam_neg", [P, 2])
        sub_g = sb("sub_g", [P, 2])
        s_lam, s_lame, s_lamn = sem("lambda_sums"), sem("lambda_exps"), sem("lambda_ready")
        INIT = [0.8 - 0.6 * math.exp(-0.3 * i) for i in (0, 3)]

        def lam_dve(dve):
            a = PARAM["lam"]
            for n in range(4):
                lo = a + n * 128
                link(dve.tensor_tensor(lamw[:, :], par[:, lo:lo + 64], par[:, lo + 64:lo + 128], ALU.mult), dve)
                ins = dve.tensor_reduce(lam_e[:, n:n + 1], lamw[:, :], AX.X, ALU.add)
                link(ins, dve)
            dve.memset(small[:, 60:61], 0.0).then_inc(s_lam, 1)
            dve.wait_ge(s_lame, 1)
            for l in range(2):
                link(dve.tensor_tensor(lam_neg[:, l:l + 1], lam_e[:, 5 + 2 * l:6 + 2 * l], lam_e[:, 4 + 2 * l:5 + 2 * l], ALU.subtract), dve)
                dve.tensor_scalar(lam_neg[:, l:l + 1], lam_neg[:, l:l + 1], -INIT[l], None, ALU.add).then_inc(s_lamn, 1)
                dve.tensor_scalar(sub_g[:, l:l + 1], g("subln", l), 1.0 - INIT[l], None, ALU.mult).then_inc(s_lamn, 1)
            dve.wait_ge(s_lamn, 4)

        def lam_act(act):
            act.wait_ge(s_lam, 1)
            act.activation(lam_e[:, 4:8], lam_e[:, 0:4], ACT.Exp).then_inc(s_lame, 1)
        stage(dve=lam_dve, act=lam_act)

        wait_x = lambda eng, k: eng.wait_ge(s_x, 16)

        def first_splits(ph, sp=None):
            def a_(act):
                for u in range(SR):
                    split_act(act, ph, u)

            def d_(dve):
                for u in range(SR):
                    split_dve(dve, ph, u)
            stage(act=a_, dve=d_, sp=sp)

        n_mix = norm_stage("mix", xts, (his, los), ("norm_mix", 0), D, eps1, wait_x, none)
        first_splits(PRE_PH)
        dests = [blocks(area(2 * i, 2)) for i in range(6)] + [u_tok[:, :, 0:256], u_tok[:, :, 256:512]]
        t_in = copy_stage("w_in", PRE_PH, pre, PRE["w_in"], "TTTTTTNN", hts, lambda pe: norm_ready(pe, n_mix), dests)

        s_conv = sem("conv_ready")

        def fft_pe(pe):
            pe.wait_ge(s_evac, t_in)
            for b in range(CB):
                for t in range(NT):
                    mm = pe.matmul(bank[b][:, :], u_tok[:, t, b * P:(b + 1) * P], dft_seq[:, t, :], start=(t == 0), stop=(t == 1))
                mm.then_inc(s_fpq, 1)
            for b in range(CB):
                pe.wait_ge(s_fpe, b + 1)
                pe.matmul(bank[4 + b][:, 0:S], dft_s[:, 1024:1152], pq[:, b, 0:S], start=True, stop=False)
                pe.matmul(bank[4 + b][:, 0:S], dft_s[:, 1152:1280], pq[:, b, S:2 * S], start=False, stop=True).then_inc(s_fy, 1)

        def fft_act(act):
            act.wait_ge(s_sum, 1)
            for b in range(CB):
                act.wait_ge(s_fpq, b + 1)
                act.activation(pq[:, b, :], bank[b][:, :], ACT.Copy).then_inc(s_fpe, 1)
            for b in range(CB):
                act.wait_ge(s_fy, b + 1)
                act.activation(yf[b], bank[4 + b][:, 0:S], ACT.Copy).then_inc(s_fpe, 1)

        def conv_dve(dve):
            dve.memset(cv[:, :, 0:1], 0.0)
            dve.memset(cv[:, :, S + 1:S + 2], 0.0)
            dve.wait_ge(s_evac, t_in)
            link(dve.tensor_tensor(cv[:, :, 1:S + 1], blocks(area(4, 4)), blocks(area(8, 4)), ALU.mult), dve)
            for b in range(CB):
                dve.tensor_scalar(yc[b], cv[:, b, 0:S], g("conv_w", b), None, ALU.mult)
            for w in (1, 2):
                link(dve.memset(small[:, 60:61], 0.0), dve)
                for b in range(CB):
                    dve.scalar_tensor_tensor(yc[b], cv[:, b, w:w + S], g("conv_w", 4 * w + b), yc[b], ALU.mult, ALU.add)
            link(dve.memset(small[:, 60:61], 0.0), dve)
            dve.tensor_tensor(blocks(area(28, 4)), blocks(area(28, 4)), blocks(area(0, 4)), ALU.mult).then_inc(s_conv, 1)
        stage(pe=fft_pe, act=fft_act, dve=conv_dve)

        n_mem = norm_stage("mem", mt, (his, los), ("norm_mem", 0), D, eps1, lambda eng, k: eng.wait_ge(s_mem, 16), none)
        copy_stage("w_k", PRE_PH, pre, PRE["w_k"], "TTTT", hts, lambda pe: norm_ready(pe, n_mem), [blocks(area(48 + 2 * i, 2)) for i in range(4)])
        copy_stage("w_v", PRE_PH, pre, PRE["w_v"], "NNNN", hts, none, [vx[:, :, i * 256:(i + 1) * 256] for i in range(4)])
        n_conv = norm_stage("conv", yc, (his[0:4], los[0:4]), ("g_conv", 0), HALF, eps1, lambda eng, k: eng.wait_ge(s_conv, 1), lambda dve: dve.wait_ge(pre_done, 16))
        n_fft = norm_stage("fft", yf, (his[4:8], los[4:8]), ("g_fft", 0), HALF, eps1, lambda eng, k: eng.wait_ge(s_fpe, CB + k + 1), none)
        t = resid_stage("w_out", PRE_PH, pre, PRE["w_out"], hts, lambda pe: norm_ready(pe, n_fft))

        n_xa = norm_stage("xattn", xts, (his, los), ("norm_xattn", 0), D, eps1, after_tiles(t), none)
        t_q = copy_stage("w_q", PRE_PH, pre, PRE["w_q"], "TTTT", hts, lambda pe: norm_ready(pe, n_xa), [blocks(area(64 + 2 * i, 2)) for i in range(4)])
        o_n = attention("xattn", 4, 1, 1,
                        lambda h, j, t_: [qx[2 * h + a][:, t_ * P:(t_ + 1) * P] for a in range(2)],
                        lambda h, j: [kx[2 * h + a] for a in range(2)],
                        lambda h, ch, part: vx[:, ch, h * 256 + part * P:h * 256 + (part + 1) * P], "two",
                        lambda n: (ht[:, 2 * n:2 * n + 2, :], hl[:, 2 * n:2 * n + 2, :]), 256 ** -0.5, lambda pe: pe.wait_ge(s_evac, t_q))
        t = resid_stage("w_o", PRE_PH, pre, PRE["w_o"], hts, lambda pe, o_n=o_n: pe.wait_ge(s_o, o_n))

        n_ffn = norm_stage("moe", xts, [area(56 + k, 1) for k in range(KB)], ("norm_ffn", 0), D, eps1, after_tiles(t), none)
        hm = area(56, 8).rearrange("p (k n) -> p k n", n=S)
        h2 = area(0, 8).rearrange("p (t n) -> p t n", t=NT)
        sel = area(12, 1).rearrange("p (t n) -> p t n", t=NT)
        selw = area(13, 1).rearrange("p (t n) -> p t n", t=NT)
        selt = area(14, 1)
        act_rows = area(16, 4)
        ys = area(24, 4)
        cut = area(28, 1).rearrange("p (a n) -> p a n", a=2)
        u1 = area(29, 1).rearrange("p (a n) -> p a n", a=2)
        sg = area(30, 1).rearrange("p (a n) -> p a n", a=2)
        gs = area(31, 1).rearrange("p (a n) -> p a n", a=2)

        def parts(a, b0, n, w):
            return a[:, b0:b0 + n, :].rearrange("p k n -> p (k n)").rearrange("p (k n) -> p k n", n=w)
        xg_hi, xg_lo = parts(ht, 0, 4, CAP), parts(hl, 0, 4, CAP)
        mh_hi, mh_lo = parts(hid_hi, 0, 4, CAP), parts(hid_lo, 0, 4, CAP)
        bias_t = parts(ht, 4, 4, 2 * CAP)
        pick = parts(hl, 4, 1, CAP)[:, 0, :]
        gt = area(32, 1)

        def rt(k, w=64):
            return big[:, 40 * 256 + k * 64:40 * 256 + k * 64 + w].rearrange("p (t n) -> p t n", t=NT)

        logit, gates, more, equal, chosen, posm, tmp = (rt(k) for k in range(7))
        top8 = big[:, 47 * 256:47 * 256 + 16].rearrange("p (t n) -> p t n", t=NT)
        st_ = big[:, 47 * 256 + 16:47 * 256 + 32]
        eqs = [big[:, 48 * 256 + k * 96:48 * 256 + k * 96 + 96].rearrange("p (t n) -> p t n", t=NT) for k in range(2)]
        lim, alim, tab = (big[:, 50 * 256 + 56 + k:50 * 256 + 57 + k] for k in range(3))
        over = big[:, 50 * 256:50 * 256 + 64]

        bgu_s = area(51, 4)
        bdn_s = area(64, 4)[0:E, :]
        rtr_s = area(55, 1)
        fours = [sem(n) for n in ("moe_const", "turned_tokens", "tokens_copied", "logits", "logit_max", "logit_exp", "gate_step", "positions", "item_list", "items_ready")]
        s_mc, s_ht, s_h2, s_lg, s_lm, s_le, s_gt, s_ps, s_il, s_items = fours
        (m_sel, m_gath, m_xhi, m_xlo, m_tsel, m_selt, m_tab, m_u1, m_cut, m_sig, m_a, m_th, m_hhi, m_hlo, m_ys, m_scat, m_add, m_gs, s_bhi, s_blo) = (
            sem("moe_" + n) for n in ("selected", "gathered", "rows_rounded", "rows_split", "selection_turned", "selection_copied",
                                      "table_loaded", "up_clamped", "gate_cut", "sigmoid", "activated", "hidden_turned", "hidden_rounded", "hidden_split",
                                      "result_copied", "scattered", "added", "gate_times_sigmoid", "bias_rounded", "bias_split"))
        moe_hi, moe_lo, moe_first = sem("moe_half_rounded"), sem("moe_half_split"), sem("moe_first_half_done")
        s_gtp, s_gtc, s_bd = sem("gates_turned"), sem("gates_copied"), sem("down_bias_done")
        s_big = sem("residual_after_moe")
        PER = 12
        HW = UW // 2
        FREE = 2 * (R - 1)

        MSR = SR + 1
        more_hi, more_lo = ([nc.alloc_sbuf_tensor_at(f"{name}{f}", [P, HW], F32R, offset=big_at + 1024 * at)[:, :] for f, at in enumerate(ats)]
                            for name, ats in (("more_hi", (8, 20)), ("more_lo", (33, 68))))

        def half(a, l, f):
            return a[:, l, f * HW:(f + 1) * HW]

        def half_hi(l, f):
            return half(w_hi, l % MSR, f) if l % MSR < SR else more_hi[f]

        def half_lo(l, f):
            return half(w_lo, l % MSR, f) if l % MSR < SR else more_lo[f]

        def used_half(eng, l, f, i):
            if l >= MSR:
                eng.wait_ge(moe_done if f else moe_first, l - MSR + 1 + i * PER)

        def round_half(act, l, f, i=0):
            if f == 0:
                act.wait_ge(moe_in[l % R], 16 * (l // R + 1) + i * (16 * PER // R))
            used_half(act, l, f, i)
            act.activation(half_hi(l, f), half(ring, l % R, f), ACT.Copy).then_inc(moe_hi, 1)

        def rest_half(dve, l, f, i=0):
            dve.wait_ge(moe_hi, 2 * l + f + 1 + i * 2 * PER)
            dve.tensor_tensor(half_lo(l, f), half(ring, l % R, f), f32(half_hi(l, f)), ALU.subtract).then_inc(moe_lo, 1)

        def gate_up(j):
            return bank[(4, 5, 2, 3)[j % 4]]

        def turned(j, n):
            at = (j // 4 * 2 + j % 2) * P
            return bank[6 + j // 2 % 2][:, at:at + n * P]

        def weights(l, f, at, n):
            return half_hi(l, f)[:, at:at + n], half_lo(l, f)[:, at:at + n]

        def wait_half(pe, l, f, i=0):
            pe.wait_ge(moe_lo, FREE + 2 * l + f + 1 + i * 2 * PER)

        def moe_sp(sp):
            sp.wait_ge(pre_done, N_PRE)
            sp.dma_start(bgu_s[:, :], bgu).then_inc(s_mc, 16)
            sp.dma_start(bdn_s[:, :], bdown).then_inc(s_mc, 16)
            sp.dma_start(rtr_s[:, :], router).then_inc(s_mc, 16)

            def load(l, i, e):
                src = wgu[e, l] if l < KB else wdn[e, l - KB]
                sp.dma_start(ring[:, l % R, :], src).then_inc(moe_in[l % R], 16)
            for l in range(PER):
                if l < R:
                    sp.wait_ge(pre_lo, N_PRE - R + 1 + (l - N_PRE % R) % R)
                else:
                    sp.wait_ge(moe_lo, FREE + 2 * (l - R + 1))
                load(l, 0, 0)
            sp.wait_ge(s_items, 1)
            n = sp.value_load(items[0:1, 0:1], min_val=E, max_val=ITEMS - 1)
            with sp.Fori(1, n) as i:
                e = sp.value_load(items[0:1, bass.ds(i + 1, 1)], min_val=0, max_val=E - 1)
                for l in range(PER):
                    sp.wait_ge(moe_lo, FREE + 2 * (l - R + 1) + i * 2 * PER)
                    src = wgu[bass.ds(e, 1), l] if l < KB else wdn[bass.ds(e, 1), l - KB]
                    sp.dma_start(ring[:, l % R, :], src.rearrange("a p n -> (a p) n")).then_inc(moe_in[l % R], 16)
            for l in range(MSR):
                sp.wait_ge(moe_lo, FREE + 2 * (l - R + 1) + n * 2 * PER)
                load(l, 0, 0)

        def moe_pe(pe):
            norm_ready(pe, n_ffn)
            for t_ in range(NT):
                for q_ in range(2):
                    for k in range(4):
                        mm = pe.transpose(bank[4 + 2 * t_ + q_][:, k * P:(k + 1) * P], hm[:, 4 * q_ + k, t_ * P:(t_ + 1) * P], ident)
                    mm.then_inc(s_ht, 1)
            pe.wait_ge(s_mc, 48)
            rw = rtr_s[:, :].rearrange("p (k n) -> p k n", n=E)
            for t_ in range(NT):
                for k in range(KB):
                    mm = pe.matmul(bank[1][:, t_ * E:(t_ + 1) * E], hm[:, k, t_ * P:(t_ + 1) * P], rw[:, k, :], start=(k == 0), stop=(k == KB - 1))
            mm.then_inc(s_lg, 1)
            pe.wait_ge(s_gt, 1)
            pe.matmul(bank[2][:, 0:E], c("before"), chosen[:, 0, :], start=True, stop=True)
            pe.matmul(bank[2][:, E:2 * E], ones, chosen[:, 0, :], start=True, stop=False)
            pe.matmul(bank[2][:, E:2 * E], c("before"), chosen[:, 1, :], start=False, stop=True)
            pe.matmul(bank[3][0:E, 0:2], chosen[:, 0, :], ones[:, 0:2], start=True, stop=False)
            pe.matmul(bank[3][0:E, 0:2], chosen[:, 1, :], ones[:, 0:2], start=False, stop=True).then_inc(s_ps, 1)
            pe.wait_ge(s_il, 1)
            pe.matmul(bank[1][0:E, 0:2], c("before")[0:E, 0:E], over[0:E, 0:2], start=True, stop=True).then_inc(s_ps, 1)
            pe.wait_ge(s_il, 2)
            pe.matmul(bank[3][0:1, 0:8], c("expert")[0:E, 0:1], over[0:E, 8:16], start=True, stop=True)
            pe.matmul(bank[1][0:1, 0:2], over[0:E, 0:1], ones[0:E, 0:2], start=True, stop=True).then_inc(s_ps, 1)
            pe.wait_ge(s_gt, 2)
            for t_ in range(NT):
                mm = pe.transpose(bank[2][0:E, t_ * P:(t_ + 1) * P], gates[:, t_, :], ident)
            mm.then_inc(s_gtp, 1)
            pe.wait_ge(s_gtc, 1)
            pe.wait_ge(s_items, 1)
            pe.wait_ge(s_h2, 4)
            n = pe.value_load(items[0:1, 0:1], min_val=E, max_val=ITEMS - 1)
            pe.wait_ge(s_blo, 1)

            def gather(value):
                pe.wait_ge(m_sel, value)
                for d in range(KB):
                    for t_ in range(NT):
                        mm = pe.matmul(bank[2 + d // 4][:, (d % 4) * CAP:(d % 4 + 1) * CAP], h2[:, t_, d * P:(d + 1) * P], sel[:, t_, :], start=(t_ == 0), stop=(t_ == 1))
                mm.then_inc(m_gath, 1)

            def turn_hidden(j, i):
                pe.wait_ge(m_a, j + 1 + i * KB)
                if j == 2:
                    pe.wait_ge(m_selt, i + 1)
                if j >= 4:
                    pe.wait_ge(m_hlo, j // 2 - 1 + i * 4)
                mm = pe.transpose(turned(j, 1), act_rows[:, j * P:(j + 1) * P], ident)
                if j % 2:
                    mm.then_inc(m_th, 1)
            gather(1)
            with pe.Fori(0, n) as i:
                for t_ in range(NT):
                    mm = pe.transpose(bank[7][:, t_ * P:(t_ + 1) * P], selw[:, t_, :], ident)
                mm.then_inc(m_tsel, 1)
                pe.wait_ge(m_xlo, 2 + i * 2)
                for j in range(KB):
                    if j < 2:
                        pe.wait_ge(m_add, j + 1 + i * 4)
                    elif j >= 4:
                        pe.wait_ge(m_gs, j - 3 + i * KB)
                    o = gate_up(j)[:, 0:2 * CAP]
                    r0 = 2 * E * (j // 4)
                    pe.matmul(o, pick[r0:r0 + 2 * E, :], bias_t[r0:r0 + 2 * E, j % 4, :], start=True, stop=False)
                    for f in range(2):
                        wait_half(pe, j, f, i)
                        mm = products(pe, o, lambda k: (xg_hi[:, k, :], xg_lo[:, k, :]), lambda k: weights(j, f, (k - f * (KB // 2)) * 256, 256), f * (KB // 2), (f + 1) * (KB // 2), False, f == 1)
                        mm.then_inc(moe_done if f else moe_first, 1)
                    if j >= 3:
                        turn_hidden(j - 3, i)
                pe.wait_ge(m_add, 4 + i * 4)
                for m in range(4):
                    pe.wait_ge(m_hlo, m + 1 + i * 4)
                    for k2 in range(2):
                        k = 2 * m + k2
                        wait_half(pe, KB + m, k2, i)
                        for hf in range(2):
                            mm = products(pe, bank[hf][:, :], lambda k_: (mh_hi[:, k, :], mh_lo[:, k, :]), lambda k_: weights(KB + m, k2, hf * 512, 512),
                                          k, k + 1, k == 0, k == KB - 1)
                        mm.then_inc(moe_done if k2 else moe_first, 1)
                    for j in ((5,), (6, 7), (), ())[m]:
                        turn_hidden(j, i)
                gather(i + 2)
                pe.wait_ge(m_ys, i + 1)
                for d in range(KB):
                    mm = pe.matmul(bank[(4, 5, 0, 1)[d // 2]][:, (d % 2) * S:(d % 2 + 1) * S], ys[:, d * P:(d + 1) * P], selt, start=True, stop=True)
                    if d % 2:
                        mm.then_inc(m_scat, 1)
            pe.wait_ge(s_bd, 1)
            for d in range(KB):
                mm = pe.matmul(bank[(2, 3, 6, 7)[d // 2]][:, (d % 2) * S:(d % 2 + 1) * S], bdn_s[:, d * P:(d + 1) * P], gt[0:E, :], start=True, stop=True)
            mm.then_inc(moe_over, 1)

        def moe_act(act):
            for q_ in range(4):
                act.wait_ge(s_ht, q_ + 1)
                act.activation(h2[:, q_ // 2, (q_ % 2) * 512:(q_ % 2 + 1) * 512], bank[4 + q_][:, :], ACT.Copy).then_inc(s_h2, 1)
            act.wait_ge(s_lm, 1)
            for t_ in range(NT):
                act.activation(gates[:, t_, :], logit[:, t_, :], ACT.Exp, bias=st_[:, 4 + t_:5 + t_]).then_inc(s_le, 1)
            act.wait_ge(s_gtp, 1)
            act.activation(gt[0:E, :], bank[2][0:E, 0:S], ACT.Copy).then_inc(s_gtc, 1)
            act.wait_ge(s_mc, 48)
            act.activation(bias_t, bgu_s.rearrange("p (k n) -> p k n", n=2 * CAP), ACT.Copy).then_inc(s_bhi, 1)
            for l in range(MSR):
                for f in range(2):
                    round_half(act, l, f)

            def rows_round(i):
                act.wait_ge(m_gath, i + 1)
                for b_ in range(2):
                    act.activation(xg_hi[:, 4 * b_:4 * b_ + 4, :], bank[2 + b_][:, :].rearrange("p (a n) -> p a n", n=CAP), ACT.Copy).then_inc(m_xhi, 1)

            def sigmoid(j, i):
                if j >= 2:
                    act.wait_ge(m_gs, j - 1 + i * KB)
                act.wait_ge(m_u1, j + 1 + i * KB)
                act.activation(cut[:, j % 2, :], gate_up(j)[:, 0:CAP], ACT.Relu, bias=lim, scale=-1.0).then_inc(m_cut, 1)
                act.wait_ge(m_cut, j + 1 + i * KB)
                act.activation(sg[:, j % 2, :], cut[:, j % 2, :], ACT.Sigmoid, bias=alim, scale=-ALPHA).then_inc(m_sig, 1)

            def hidden_round(p, i):
                act.wait_ge(m_th, p + 1 + i * 4)
                if p >= 2:
                    act.wait_ge(m_hlo, p - 1 + i * 4)
                act.activation(mh_hi[:, 2 * p:2 * p + 2, :], turned(2 * p, 2).rearrange("p (a n) -> p a n", a=2), ACT.Copy).then_inc(m_hhi, 1)
            rows_round(0)
            act.wait_ge(s_items, 1)
            n = act.value_load(items[0:1, 0:1], min_val=E, max_val=ITEMS - 1)
            with act.Fori(0, n) as i:
                act.activation(tab, eps1[:, 0:1], ACT.Sigmoid).then_inc(m_tab, 1)
                act.wait_ge(m_tab, i + 1)
                act.wait_ge(m_tsel, i + 1)
                act.activation(selt, bank[7][:, 0:S], ACT.Copy).then_inc(m_selt, 1)
                for j in range(KB):
                    for f in range(2):
                        if j < KB - 1:
                            round_half(act, j + MSR, f, i)
                    if j:
                        sigmoid(j - 1, i)
                    if j % 2 and j >= 5:
                        hidden_round(j // 2 - 2, i)
                sigmoid(KB - 1, i)
                for l in range(KB - 1, PER - 1):
                    if l < KB + 1:
                        hidden_round(l - KB + 3, i)
                    for f in range(2):
                        round_half(act, l + MSR, f, i)
                round_half(act, PER - 1 + MSR, 0, i)
                act.wait_ge(moe_done, PER + i * PER)
                act.activation(ys[:, 0:512], bank[0][:, :], ACT.Copy)
                act.activation(ys[:, 512:1024], bank[1][:, :], ACT.Copy).then_inc(m_ys, 1)
                round_half(act, PER - 1 + MSR, 1, i)
                rows_round(i + 1)

        def moe_dve(dve):
            dve.sem_inc(moe_lo, FREE)
            dve.wait_ge(s_mc, 48)
            dve.memset(lim, LIMIT)
            dve.memset(alim, ALPHA * LIMIT)
            dve.wait_ge(s_lg, 1)
            br = par[:, PARAM["b_router"]:PARAM["b_router"] + 64].rearrange("p (t n) -> p t n", t=NT)
            link(dve.tensor_tensor(logit, bank[1][:, 0:64].rearrange("p (t n) -> p t n", t=NT), br, ALU.add), dve)
            for t_ in range(NT):
                ins = dve.max(top8[:, t_, :], logit[:, t_, :])
            link(ins, dve)
            for t_ in range(NT):
                dve.tensor_scalar(st_[:, 4 + t_:5 + t_], top8[:, t_, 0:1], -1.0, None, ALU.mult).then_inc(s_lm, 1) if t_ else \
                    dve.tensor_scalar(st_[:, 4 + t_:5 + t_], top8[:, t_, 0:1], -1.0, None, ALU.mult)
            for k in range(2):
                dve.memset(eqs[k], 0.0)
            for t_ in range(NT):
                ins = dve.tensor_scalar(more[:, t_, :], logit[:, t_, :], top8[:, t_, TOP - 1:TOP], None, ALU.is_gt)
            link(ins, dve)
            for t_ in range(NT):
                dve.tensor_scalar(equal[:, t_, :], logit[:, t_, :], top8[:, t_, TOP - 1:TOP], None, ALU.is_equal)
                dve.tensor_scalar(eqs[0][:, t_, 16:48], logit[:, t_, :], top8[:, t_, TOP - 1:TOP], None, ALU.is_equal)
            link(dve.tensor_reduce(st_[:, 0:2], more, AX.X, ALU.add), dve)
            ins = dve.tensor_scalar(st_[:, 0:2], st_[:, 0:2], -1.0, float(TOP), ALU.mult, ALU.add)
            link(ins, dve)
            cur = 0
            for sh in (1, 2, 4, 8, 16):
                link(dve.tensor_tensor(eqs[1 - cur][:, :, 16:48], eqs[cur][:, :, 16:48], eqs[cur][:, :, 16 - sh:48 - sh], ALU.add), dve)
                cur = 1 - cur
            for t_ in range(NT):
                ins = dve.scalar_tensor_tensor(tmp[:, t_, :], eqs[cur][:, t_, 16:48], st_[:, t_:t_ + 1], equal[:, t_, :], ALU.is_le, ALU.mult)
            link(ins, dve)
            link(dve.tensor_tensor(chosen, tmp, more, ALU.add), dve)
            dve.memset(over[:, 60:61], 0.0).then_inc(s_gt, 1)
            dve.wait_ge(s_le, 2)
            link(dve.tensor_tensor(gates, gates, chosen, ALU.mult), dve)
            link(dve.tensor_reduce(st_[:, 8:10], gates, AX.X, ALU.add), dve)
            link(dve.reciprocal(st_[:, 10:12], st_[:, 8:10]), dve)
            for t_ in range(NT):
                ins = dve.tensor_scalar(gates[:, t_, :], gates[:, t_, :], st_[:, 10 + t_:11 + t_], None, ALU.mult)
            link(ins, dve)
            dve.memset(over[:, 60:61], 0.0).then_inc(s_gt, 1)
            dve.wait_ge(s_ps, 1)
            link(dve.tensor_scalar(tmp, bank[2][:, 0:64].rearrange("p (t n) -> p t n", t=NT), 1.0, None, ALU.add), dve)
            link(dve.tensor_tensor(tmp, tmp, chosen, ALU.mult), dve)
            link(dve.tensor_scalar(posm, tmp, -1.0, None, ALU.add), dve)
            dve.tensor_scalar(over[0:E, 0:2], bank[3][0:E, 0:2], float(CAP), None, ALU.is_gt).then_inc(s_il, 1)
            dve.wait_ge(s_ps, 2)
            link(dve.tensor_copy(over[0:E, 4:5], bank[1][0:E, 0:1]), dve)
            dve.tensor_scalar(over[0:E, 8:16], c("slot")[0:E, 0:8], over[0:E, 4:5], over[0:E, 0:1], ALU.is_equal, ALU.mult).then_inc(s_il, 1)
            dve.wait_ge(s_ps, 3)
            dve.tensor_scalar(items[0:1, 0:1], bank[1][0:1, 0:1], float(E), None, ALU.add)
            dve.tensor_copy(items[0:1, 1:1 + E], c("slot")[0:1, 0:E])
            dve.tensor_copy(items[0:1, 1 + E:1 + ITEMS], bank[3][0:1, 0:8])
            dve.memset(items[0:1, 1 + ITEMS:1 + ITEMS + E], 0)
            link(dve.memset(items[0:1, 1 + ITEMS + E:1 + 2 * ITEMS], CAP), dve)
            dve.memset(over[:, 60:61], 0.0).then_inc(s_items, 1)
            dve.sem_inc(m_add, 4)
            dve.wait_ge(s_bhi, 1)
            for r0 in (E, 3 * E):
                o = bias_t[r0:r0 + E]
                ins = dve.tensor_tensor(o, bgu_s[r0:r0 + E].rearrange("p (k n) -> p k n", n=2 * CAP), f32(o), ALU.subtract)
            ins.then_inc(s_blo, 1)
            for l in range(MSR):
                for f in range(2):
                    rest_half(dve, l, f)
            dve.wait_ge(s_items, 1)
            n = dve.value_load(items[0:1, 0:1], min_val=E, max_val=ITEMS - 1)

            def select(i, first=False):
                if first:
                    e, r0 = 0, 0
                else:
                    e = dve.value_load(items[0:1, bass.ds(i + 1, 1)], min_val=0, max_val=E - 1)
                    r0 = dve.value_load(items[0:1, bass.ds(i + 1 + ITEMS, 1)], min_val=0, max_val=CAP)
                for t_ in range(NT):
                    pc = posm[:, t_, 0:1] if first else big[:, bass.ds(40 * 256 + 5 * 64 + t_ * 32 + e, 1)]
                    gc = gates[:, t_, 0:1] if first else big[:, bass.ds(40 * 256 + 64 + t_ * 32 + e, 1)]
                    rows = c("slot")[:, 0:CAP] if first else con[:, bass.ds(CONST["slot"][0] + r0, CAP)]
                    dve.tensor_scalar(sel[:, t_, :], rows, pc, None, ALU.is_equal)
                    dve.tensor_scalar(selw[:, t_, :], rows, pc, gc, ALU.is_equal, ALU.mult)
                mc = c("mod32")[:, 0:1] if first else con[:, bass.ds(CONST["mod32"][0] + e, 1)]
                dve.tensor_scalar(pick, ones, mc, None, ALU.mult).then_inc(m_sel, 1)
            select(0, True)

            def rows_rest(i):
                for b_ in range(2):
                    dve.wait_ge(m_xhi, 1 + b_ + i * 2)
                    o = xg_hi[:, 4 * b_:4 * b_ + 4, :]
                    dve.tensor_tensor(xg_lo[:, 4 * b_:4 * b_ + 4, :], bank[2 + b_][:, :].rearrange("p (a n) -> p a n", n=CAP), f32(o), ALU.subtract).then_inc(m_xlo, 1)

            def hidden_rest(p, i):
                dve.wait_ge(m_hhi, p + 1 + i * 4)
                dve.tensor_tensor(mh_lo[:, 2 * p:2 * p + 2, :], turned(2 * p, 2).rearrange("p (a n) -> p a n", a=2), f32(mh_hi[:, 2 * p:2 * p + 2, :]), ALU.subtract).then_inc(m_hlo, 1)

            def activate(j, i):
                dve.wait_ge(m_gs, j + 1 + i * KB)
                dve.scalar_tensor_tensor(act_rows[:, j * P:(j + 1) * P], u1[:, j % 2, :], 1.0, gs[:, j % 2, :], ALU.add, ALU.mult).then_inc(m_a, 1)

            def gate_times_sigmoid(j, i):
                dve.wait_ge(m_sig, j + 1 + i * KB)
                dve.scalar_tensor_tensor(gs[:, j % 2, :], gate_up(j)[:, 0:CAP], LIMIT, sg[:, j % 2, :], ALU.min, ALU.mult).then_inc(m_gs, 1)
            rows_rest(0)
            with dve.Fori(0, n) as i:
                for j in range(KB):
                    if j < KB - 1:
                        rest_half(dve, j + MSR, 0, i)
                    if j >= 2:
                        activate(j - 2, i)
                    if j >= 6:
                        hidden_rest(j - 6, i)
                    if j < KB - 1:
                        rest_half(dve, j + MSR, 1, i)
                    if j:
                        gate_times_sigmoid(j - 1, i)
                    if j >= 2:
                        dve.wait_ge(m_a, j - 1 + i * KB)
                    dve.wait_ge(moe_done, j + 1 + i * PER)
                    dve.tensor_scalar(u1[:, j % 2, :], gate_up(j)[:, CAP:2 * CAP], LIMIT, -LIMIT, ALU.min, ALU.max).then_inc(m_u1, 1)
                activate(KB - 2, i)
                gate_times_sigmoid(KB - 1, i)
                activate(KB - 1, i)
                for l in range(KB - 1, PER):
                    if l < KB + 1:
                        hidden_rest(l - KB + 3, i)
                    for f in range(2):
                        rest_half(dve, l + MSR, f, i)
                    if l == KB:
                        dve.wait_ge(m_tsel, i + 1)
                        select(i + 1)
                rows_rest(i + 1)
                for b_ in range(4):
                    dve.wait_ge(m_scat, b_ + 1 + i * 4)
                    o = xt[:, 2 * b_:2 * b_ + 2, :]
                    dve.tensor_tensor(o, o, bank[(4, 5, 0, 1)[b_]][:, :].rearrange("p (a n) -> p a n", a=2), ALU.add).then_inc(m_add, 1)
            dve.memset(over[:, 60:61], 0.0).then_inc(s_bd, 1)
            dve.wait_ge(moe_over, 1)
            for b_ in range(4):
                o = xt[:, 2 * b_:2 * b_ + 2, :]
                dve.tensor_tensor(o, o, bank[(2, 3, 6, 7)[b_]][:, :].rearrange("p (a n) -> p a n", a=2), ALU.add).then_inc(s_big, 1)
        stage(pe=moe_pe, act=moe_act, dve=moe_dve, sp=moe_sp)
        moe_stage = lambda eng, k: eng.wait_ge(s_big, k // 2 + 1)
        first_splits(POST_PH)
        n_fin = norm_stage("first_final", xts, xts, ("norm_final", 0), D, eps1, moe_stage, none)

        src_wait = lambda eng, k: norm_ready(eng, n_fin, k)
        sl = dict(sq=sem("subln_squared"), sm=sem("subln_summed"), rt=sem("subln_root"), rd=sem("subln_ready"), nm=sem("subln_scaled"), hi=sem("subln_rounded"))
        sl_n = [0]
        for l in range(4):
            n_a = norm_stage(f"attn{l}", xts, (his, los), ("attn", 8 * l), D, eps2, src_wait, none)
            a_ready = lambda pe, n_a=n_a: norm_ready(pe, n_a)
            if l in (0, 3):
                lam = 0 if l == 0 else 1
                spec = [("T", True, 2 * i) for i in range(8)] + [("N", False, (16, i)) for i in range(4)]
                t = rope_stage(f"a_qkv{l}", POST_PH, post, POST["a_qkv", l], [(*x_, 0) for x_ in spec], hts, a_ready, c("rot_ac"), c("cs_ac"))
                va = area(16, 8).rearrange("p (t n) -> p t n", t=NT)
                oa = [area(24 + h, 1) for h in range(8)]
                o_n = attention(f"a{l}", 8, 1, 2,
                                lambda h, j, t_: [area(h, 1)[64 * j:64 * j + 64, t_ * P:(t_ + 1) * P]],
                                lambda h, j: [area(8 + h, 1)[64 * j:64 * j + 64, :]],
                                lambda h, ch, part: va[:, ch, h * P:(h + 1) * P], "one",
                                lambda n: oa[n], 64 ** -0.5, lambda pe, t=t: pe.wait_ge(s_evac, t), coef=lam_neg[:, lam:lam + 1])

                def sub_act(act, k=sl_n[0], o_n=o_n):
                    for h in range(8):
                        act.wait_ge(s_o, o_n - 8 + h + 1)
                        act.activation(sq[:, h, :], oa[h], ACT.Square).then_inc(sl["sq"], 1)
                    for b in range(4):
                        act.wait_ge(sl["sm"], 4 * k + b + 1)
                        act.activation(area(32 + 2 * b, 2), bank[b][:, :], ACT.Sqrt, bias=eps2[:, 0:1], scale=1.0 / P).then_inc(sl["rt"], 1)
                    for h in range(8):
                        act.wait_ge(sl["nm"], 8 * k + h + 1)
                        act.activation(his[h], oa[h], ACT.Copy).then_inc(sl["hi"], 1)

                def sub_pe(pe, k=sl_n[0], o_n=o_n):
                    pe.wait_ge(s_o, o_n)
                    for h in range(8):
                        pe.wait_ge(sl["sq"], 8 * k + h + 1)
                        mm = pe.matmul(bank[h // 2][:, (h % 2) * S:(h % 2 + 1) * S], ones, sq[:, h, :], start=True, stop=True)
                        if h % 2:
                            mm.then_inc(sl["sm"], 1)

                def sub_dve(dve, k=sl_n[0], lam=lam):
                    for b in range(4):
                        dve.wait_ge(sl["rt"], 4 * k + b + 1)
                        link(dve.reciprocal(area(32 + 2 * b, 2), area(32 + 2 * b, 2)), dve)
                        for h in (2 * b, 2 * b + 1):
                            dve.scalar_tensor_tensor(oa[h], oa[h], sub_g[:, lam:lam + 1], area(32 + h, 1), ALU.mult, ALU.mult).then_inc(sl["nm"], 1)
                    for h in range(8):
                        dve.wait_ge(sl["hi"], 8 * k + h + 1)
                        dve.tensor_tensor(los[h], oa[h], f32(his[h]), ALU.subtract).then_inc(sl["rd"], 1)
                sl_n[0] += 1
                stage(act=sub_act, pe=sub_pe, dve=sub_dve)
                t = resid_stage(f"a_o{l}", POST_PH, post, POST["a_o", l], hts, lambda pe, n=sl_n[0]: pe.wait_ge(sl["rd"], 8 * n))
            elif l == 1:
                t = copy_stage("b_a", POST_PH, post, POST["b_a", l], "TTT", hts, a_ready, [blocks(area(2 * i, 2)) for i in range(3)])
                lat = lambda eng, k, t=t: eng.wait_ge(s_evac, t)
                s_kr, s_krd = sem("k_rope_rotated"), sem("k_rope_ready")

                def kr_pe(pe, t=t):
                    pe.wait_ge(s_evac, t)
                    pe.matmul(bank[1][:, 0:S], c("rot_b"), area(5, 1), start=True, stop=True).then_inc(s_kr, 1)

                def kr_dve(dve):
                    dve.wait_ge(s_kr, 1)
                    dve.tensor_tensor(area(14, 1), area(5, 1), c("cs_b")[:, 0:S], ALU.mult)
                    link(dve.tensor_tensor(area(15, 1), bank[1][:, 0:S], c("cs_b")[:, 512:512 + S], ALU.mult), dve)
                    dve.tensor_tensor(area(6, 1), area(14, 1), area(15, 1), ALU.add).then_inc(s_krd, 1)
                    dve.wait_ge(s_krd, 1)
                stage(pe=kr_pe, dve=kr_dve)
                n_q = norm_stage("b_q", [area(k, 1) for k in range(3)], (his[0:3], los[0:3]), ("q_norm", 0), 384, eps2, lat, none)
                n_kv = norm_stage("b_kv", [area(3 + k, 1) for k in range(2)], (his[3:5], los[3:5]), ("kv_norm", 0), 256, eps2, lat, none)
                spec = [("T", i >= 4, 16 + 2 * i, 0) for i in range(6)]
                rope_stage("b_qb", POST_PH, post, POST["b_q", l], spec, hts[0:3], lambda pe, n=n_q: norm_ready(pe, n), c("rot_b"), c("cs_b"), kc=3)
                kvs = hts[3:5]
                copy_stage("b_k", POST_PH, post, POST["b_k", l], "TTTT", kvs, lambda pe, n=n_kv: norm_ready(pe, n), [blocks(area(28 + 2 * i, 2)) for i in range(4)], kc=2)
                vb = area(36, 8).rearrange("p (t n) -> p t n", t=NT)
                t = copy_stage("b_v", POST_PH, post, POST["b_v", l], "NNNN", kvs, none, [vb[:, :, i * 256:(i + 1) * 256] for i in range(4)], kc=2)
                quad = [0, 2, 1, 3]
                o_n = attention("b", 16, 1, 1,
                                lambda h, j, t_: [area(16 + h // 2, 1)[64 * (h % 2):64 * (h % 2) + 64, t_ * P:(t_ + 1) * P],
                                                  area(24 + h // 4, 1)[32 * quad[h % 4]:32 * quad[h % 4] + 32, t_ * P:(t_ + 1) * P]],
                                lambda h, j: [area(28 + h // 2, 1)[64 * (h % 2):64 * (h % 2) + 64, :], area(6, 1)[32 * quad[h % 4]:32 * quad[h % 4] + 32, :]],
                                lambda h, ch, part: vb[:, ch, h * 64:h * 64 + 64], "half",
                                lambda n: hts[n], 96 ** -0.5, lambda pe, t=t: pe.wait_ge(s_evac, t))
                t = resid_stage("b_o", POST_PH, post, POST["b_o", l], hts, lambda pe, o_n=o_n: pe.wait_ge(s_o, o_n))
            else:
                spec = [("T", True, 2 * i, 0) for i in range(4)] + [("T", True, 24 + 2 * i, 0) for i in range(4)] + [("N", False, (48, i), 0) for i in range(4)]
                t = rope_stage("c_qkv", POST_PH, post, POST["c_qkv", l], spec, hts, a_ready, c("rot_ac"), c("cs_ac"), times=3, step=8)
                vc = [area(48 + 8 * j, 8).rearrange("p (t n) -> p t n", t=NT) for j in range(3)]
                masks = [c(f"mask{j}") for j in range(3)]
                o_n = attention("c", 16, 3, 1,
                                lambda h, j, t_: [area(8 * j + h // 2, 1)[64 * (h % 2):64 * (h % 2) + 64, t_ * P:(t_ + 1) * P]],
                                lambda h, j: [area(24 + 8 * j + h // 2, 1)[64 * (h % 2):64 * (h % 2) + 64, :]],
                                lambda h, ch, part: vc[ch // 2][:, ch % 2, h * 64:h * 64 + 64], "half",
                                lambda n: hts[n], 64 ** -0.5, lambda pe, t=t: pe.wait_ge(s_evac, t), masks=masks)
                t = resid_stage("c_o", POST_PH, post, POST["c_o", l], hts, lambda pe, o_n=o_n: pe.wait_ge(s_o, o_n))
            n_f = norm_stage(f"ffn{l}", xts, (his, los), ("ffn", 8 * l), D, eps2, after_tiles(t), none)
            t = ffn_stage(l, lambda pe, n_f=n_f: norm_ready(pe, n_f))
            src_wait = after_tiles(t)
        n_last = norm_stage("last", xts, [area(k, 1) for k in range(KB)], ("final2", 0), D, eps2, src_wait, none)

        def last_sp(sp):
            norm_ready(sp, n_last)
            sp.dma_start(out, blocks(area(0, 8))).then_inc(s_out, 16)
            sp.wait_ge(s_out, 16)
        stage(sp=last_sp)

        @block.sync
        def _(sp):
            for st in STAGES:
                if st["sp"]:
                    st["sp"](sp)

        @block.tensor
        def _(pe):
            for st in STAGES:
                if st["pe"]:
                    st["pe"](pe)

        @block.scalar
        def _(act):
            for st in STAGES:
                if st["act"]:
                    st["act"](act)

        @block.vector
        def _(dve):
            for st in STAGES:
                if st["dve"]:
                    st["dve"](dve)


_PARAMS = ["x", "mem", "norm_mix", "w_in", "conv_w", "g_conv_out", "g_fft_out", "w_out", "norm_xattn", "norm_mem", "w_q",
           "w_k", "w_v", "w_o", "norm_ffn", "w_router", "b_router", "w_gate_up", "b_gate_up", "w_down", "b_down",
           "norm_final"]


def lay_out(inputs):
    a = {k: np.asarray(v) for k, v in inputs.items()}

    def channels(v):
        return np.ascontiguousarray(v.reshape(S, KB, P).transpose(2, 1, 0))

    def col(v):
        return v.reshape(-1, P).T

    def rep(v):
        return np.broadcast_to(v.reshape(1, -1), (P, v.size))

    def units(w, names=None):
        K, N = w.shape
        u = w.reshape(K // P, P, N // 256, 256).transpose(2, 1, 0, 3).reshape(N // 256, P, -1)
        out = np.zeros((u.shape[0], P, UW), np.float32)
        out[:, :, :u.shape[2]] = u
        return list(out)

    pre = []
    for n in ("w_in", "w_k", "w_v", "w_out", "w_q", "w_o"):
        pre += units(a[n][0])

    def gate_up(w, f):
        return w.reshape(KB, P, 2, f // P, P).transpose(3, 1, 0, 2, 4).reshape(f // P, P, UW)

    def rows(w):
        return w.reshape(-1, 2, P, D).transpose(0, 2, 1, 3).reshape(-1, P, UW)

    post = []
    for l in range(4):
        if l in (0, 3):
            post += units(a["a_w_qkv_2"][l // 3]) + units(a["a_w_o_2"][l // 3])
        elif l == 1:
            w = a["b_w_a_2"][0]
            post += units(np.concatenate([w[:, :640], w[:, 640:], w[:, 640:], w[:, 640:], w[:, 640:]], 1))
            q = a["b_w_qb_2"][0].reshape(384, 16, 96)
            order = [4 * b + o for b in range(4) for o in (0, 2, 1, 3)]
            post += units(np.concatenate([q[:, :, :64].reshape(384, 1024), q[:, order, 64:].reshape(384, 512)], 1))
            kv = a["b_w_kvb_2"][0].reshape(256, 16, 128)
            post += units(kv[:, :, :64].reshape(256, 1024)) + units(kv[:, :, 64:].reshape(256, 1024))
            post += units(a["b_w_o_2"][0])
        else:
            post += units(a["c_w_qkv_2"][0]) + units(a["c_w_o_2"][0])
        gu, dn = gate_up(a["f_w_gu_2"][l], FB * P), rows(a["f_w_out_2"][l])
        post += [gu[0], gu[1]]
        for j in range(1, FB // 2):
            post += [gu[2 * j], gu[2 * j + 1], dn[j - 1]]
        post.append(dn[FB // 2 - 1])
    lam = np.concatenate([a[f"a_lambda_{n}_2"][l] for l in range(2) for n in ("q1", "k1", "q2", "k2")])
    params = np.concatenate([
        col(a["norm_mix"][0]), col(a["norm_mem"][0]), col(a["norm_xattn"][0]), col(a["norm_ffn"][0]), col(a["norm_final"]),
        col(a["g_conv_out"][0]), col(a["g_fft_out"][0]), col(a["conv_w"][0].reshape(-1)), col(a["attn_norm_2"].reshape(-1)),
        col(a["ffn_norm_2"].reshape(-1)), col(a["final_norm_2"]), col(a["b_q_norm_2"].reshape(-1)), col(a["b_kv_norm_2"].reshape(-1)),
        col(a["a_subln_2"].reshape(-1)), rep(np.concatenate([a["b_router"][0]] * 2)), rep(lam)], 1)
    return {
        "xin": channels(a["x"][0]), "memin": channels(a["mem"][0]), "consts": CONSTS, "dft": DFT, "params": params,
        "pre": np.stack(pre), "post": np.stack(post),
        "router": a["w_router"][0].reshape(KB, P, E).transpose(1, 0, 2).reshape(P, -1),
        "bgu": a["b_gate_up"][0].reshape(E, 2, 2, 4, P).transpose(2, 0, 3, 1, 4).reshape(2, 1, E, D).repeat(2, 1).reshape(P, D),
        "bdown": a["b_down"][0],
        "wgu": a["w_gate_up"][0].reshape(E, KB, P, 2, KB, P).transpose(0, 4, 2, 1, 3, 5).reshape(E, KB, P, UW),
        "wdn": a["w_down"][0].reshape(E, 4, 2, P, D).transpose(0, 1, 3, 2, 4).reshape(E, 4, P, UW),
    }


def kernel(**inputs):
    import concourse.bacc as bacc
    from concourse.bass_utils import run_bass_kernel_spmd
    arrays = {n: np.ascontiguousarray(v) for n, v in lay_out(inputs).items()}
    nc = bacc.Bacc("TRN2", target_bir_lowering=False, num_devices=1)
    aps = {n: nc.dram_tensor(n, v.shape, F32, kind="ExternalInput").ap() for n, v in arrays.items()}
    out = nc.dram_tensor("out", (P, KB, S), F32, kind="ExternalOutput").ap()
    program(nc, aps["xin"], aps["memin"], aps["consts"], aps["dft"], aps["params"], aps["pre"], aps["post"],
            aps["router"], aps["bgu"], aps["bdown"], aps["wgu"], aps["wdn"], out)
    r = run_bass_kernel_spmd(nc, [arrays], core_ids=[0])
    got = r.results[0]["out"]
    return np.ascontiguousarray(got.transpose(2, 1, 0)).reshape(1, S, D)
```
